# Optimizing a Trainium2 kernel written in Bass

```python
import jax, jax.numpy as jnp
from jax import lax
import numpy as np

D_MODEL = 1024
BATCH = 1
SEQ = 512
DEPTH = 2

DIL_GROUPS = ((128, 1), (512, 4), (2048, 16))
N_GROUPS = 3
A_HEADS = 8
A_HEAD_DIM = 64
A_WIDTH = N_GROUPS * A_HEADS * A_HEAD_DIM
A_OUT = A_HEADS * A_HEAD_DIM
ROT_DIM = A_HEAD_DIM // 4
ROPE_THETA = 500000.0
ATT_BLOCK = 128
NEG_INF = -1e30
R_HEADS = 4
R_KEY_DIM = 128
R_VAL_DIM = 256
R_QK = R_HEADS * R_KEY_DIM
R_V = R_HEADS * R_VAL_DIM
R_CHUNK = 128
R_ROT_BASE = 10000.0
D_FF = 4 * D_MODEL
NORM_EPS = 1e-6

_SIZES = (A_WIDTH, A_WIDTH, A_WIDTH, R_QK, R_QK, R_V, R_V, D_MODEL, D_MODEL)
D_IN = sum(_SIZES)
SPLIT_POINTS = tuple(sum(_SIZES[:i + 1]) for i in range(len(_SIZES) - 1))

kernel_name = "dilated_attn_retention_gated_hybrid"

def rmsnorm(x, g):
    xf = x.astype(jnp.float32)
    y = xf * lax.rsqrt(jnp.mean(xf * xf, axis=-1, keepdims=True) + NORM_EPS)
    return (y * g.astype(jnp.float32)).astype(x.dtype)

def rotary(x, pos, rot_dim, base):
    half = rot_dim // 2
    inv = 1.0 / (base ** (jnp.arange(half, dtype=jnp.float32) / half))
    ang = pos.astype(jnp.float32)[:, None] * inv[None, :]
    cos = jnp.cos(ang)[None, :, None, :]
    sin = jnp.sin(ang)[None, :, None, :]
    xr = x[..., :rot_dim].astype(jnp.float32)
    x1, x2 = xr[..., :half], xr[..., half:]
    rot = jnp.concatenate([x1 * cos - x2 * sin, x1 * sin + x2 * cos], axis=-1).astype(x.dtype)
    return jnp.concatenate([rot, x[..., rot_dim:]], axis=-1)

def dilated_group_attention(q, k, v, window, dilation):
    b, s, h, dh = q.shape
    span = dilation * ATT_BLOCK
    L = -(-s // span) * span
    n_sub = L // dilation
    nb = n_sub // ATT_BLOCK
    reach = window // dilation

    def to_blocks(t):
        t = jnp.pad(t, ((0, 0), (0, L - s), (0, 0), (0, 0)))
        t = t.reshape(b, n_sub, dilation, h, dh).transpose(0, 2, 3, 1, 4)
        return t.reshape(b, dilation, h, nb, ATT_BLOCK, dh)

    def with_prev(t):
        prev = jnp.pad(t, ((0, 0), (0, 0), (0, 0), (1, 0), (0, 0), (0, 0)))[:, :, :, :-1]
        return jnp.concatenate([prev, t], axis=-2)

    qb, kb, vb = to_blocks(q), to_blocks(k), to_blocks(v)
    kk, vv = with_prev(kb), with_prev(vb)
    scores = jnp.einsum('brhnqd,brhnkd->brhnqk', qb, kk).astype(jnp.float32) * (dh ** -0.5)
    qi = jnp.arange(ATT_BLOCK)[:, None]
    kj = jnp.arange(2 * ATT_BLOCK)[None, :]
    dist = qi + ATT_BLOCK - kj
    band = (dist >= 0) & (dist <= reach)
    blk = jnp.arange(nb)[:, None, None]
    mask = band[None] & ((blk > 0) | (kj >= ATT_BLOCK)[None])
    scores = jnp.where(mask, scores, NEG_INF)
    m = jnp.max(scores, axis=-1, keepdims=True)
    p = jnp.exp(scores - m)
    den = jnp.sum(p, axis=-1, keepdims=True)
    out = jnp.einsum('brhnqk,brhnkd->brhnqd', (p / den).astype(v.dtype), vv)
    lse = (m + jnp.log(den))[..., 0]

    def from_blocks(t):
        rest = t.shape[5:]
        t = t.reshape((b, dilation, h, n_sub) + rest)
        t = jnp.moveaxis(t, 3, 1)
        return t.reshape((b, L, h) + rest)[:, :s]

    return from_blocks(out), from_blocks(lse)

def retention(q, k, v):
    b, s, h, dk = q.shape
    dv = v.shape[-1]
    nc = s // R_CHUNK
    C = R_CHUNK
    lg = jnp.log1p(-(2.0 ** (-5.0 - jnp.arange(h, dtype=jnp.float32))))

    def chunks(t, d):
        return t.astype(jnp.float32).reshape(b, nc, C, h, d).transpose(0, 3, 1, 2, 4)

    qc = chunks(q, dk)
    kc = chunks(k, dk) * (dk ** -0.5)
    vc = chunks(v, dv)
    idx = jnp.arange(C, dtype=jnp.float32)
    diff = idx[:, None] - idx[None, :]
    decay = jnp.where(diff >= 0, jnp.exp(diff[None] * lg[:, None, None]), 0.0)
    zeta = jnp.exp((C - 1 - idx)[None, :] * lg[:, None])
    xi = jnp.exp((idx + 1)[None, :] * lg[:, None])
    chunk_decay = jnp.exp(C * lg)[None, :, None, None]

    inner_s = jnp.einsum('bhncd,bhnmd->bhncm', qc, kc) * decay[None, :, None]
    inner = jnp.einsum('bhncm,bhnme->bhnce', inner_s, vc)
    kv = jnp.einsum('bhncd,bhnce->bhnde', kc * zeta[None, :, None, :, None], vc)

    def step(state, kv_i):
        return state * chunk_decay + kv_i, state

    _, prev_states = lax.scan(step, jnp.zeros((b, h, dk, dv), jnp.float32), jnp.moveaxis(kv, 2, 0))
    prev_states = jnp.moveaxis(prev_states, 0, 2)
    cross = jnp.einsum('bhncd,bhnde->bhnce', qc * xi[None, :, None, :, None], prev_states)
    out = inner + cross
    return out.transpose(0, 2, 3, 1, 4).reshape(b, s, h, dv)

def hybrid_layer(x, g_mix, w_in, w_a, w_b, w_o, g_ffn, w_up, w_down):
    b, s, _ = x.shape
    pos = jnp.arange(s)
    hn = rmsnorm(x, g_mix)
    proj = hn @ w_in
    qa, ka, va, qr, kr, vr, gr, ga, gb = jnp.split(proj, SPLIT_POINTS, axis=-1)

    def heads_a(t):
        return t.reshape(b, s, N_GROUPS * A_HEADS, A_HEAD_DIM)
    qa = rotary(heads_a(qa), pos, ROT_DIM, ROPE_THETA).reshape(b, s, N_GROUPS, A_HEADS, A_HEAD_DIM)
    ka = rotary(heads_a(ka), pos, ROT_DIM, ROPE_THETA).reshape(b, s, N_GROUPS, A_HEADS, A_HEAD_DIM)
    va = va.reshape(b, s, N_GROUPS, A_HEADS, A_HEAD_DIM)
    outs, lses = [], []
    for gi, (window, dilation) in enumerate(DIL_GROUPS):
        o, l = dilated_group_attention(qa[:, :, gi], ka[:, :, gi], va[:, :, gi], window, dilation)
        outs.append(o.astype(jnp.float32))
        lses.append(l)
    wts = jax.nn.softmax(jnp.stack(lses, axis=0), axis=0)
    y_a = jnp.sum(wts[..., None] * jnp.stack(outs, axis=0), axis=0).astype(x.dtype)
    y_a = y_a.reshape(b, s, A_OUT) @ w_a

    qr = rotary(qr.reshape(b, s, R_HEADS, R_KEY_DIM), pos, R_KEY_DIM, R_ROT_BASE)
    kr = rotary(kr.reshape(b, s, R_HEADS, R_KEY_DIM), pos, R_KEY_DIM, R_ROT_BASE)
    ret = retention(qr, kr, vr.reshape(b, s, R_HEADS, R_VAL_DIM))
    ret = ret * lax.rsqrt(jnp.mean(ret * ret, axis=-1, keepdims=True) + NORM_EPS)
    y_b = (jax.nn.silu(gr.astype(jnp.float32)) * ret.reshape(b, s, R_V)).astype(x.dtype) @ w_b

    merged = jax.nn.sigmoid(ga) * y_a + jax.nn.sigmoid(gb) * y_b
    x = x + merged @ w_o

    h2 = rmsnorm(x, g_ffn)
    x = x + jnp.square(jax.nn.relu(h2 @ w_up)) @ w_down
    return x

def setup_inputs(seed: int = 0) -> dict:
    key = jax.random.key(seed)
    ks = jax.random.split(key, 10)
    f32 = jnp.float32

    def w(k, shape, fan_in):
        return jax.random.normal(k, shape, f32) * (fan_in ** -0.5)

    def gain(k, shape):
        return 1.0 + 0.05 * jax.random.normal(k, shape, f32)

    return {
        "x": jax.random.normal(ks[0], (BATCH, SEQ, D_MODEL), f32),
        "mix_norm": gain(ks[1], (DEPTH, D_MODEL)),
        "w_in": w(ks[2], (DEPTH, D_MODEL, D_IN), D_MODEL),
        "w_a": w(ks[3], (DEPTH, A_OUT, D_MODEL), A_OUT),
        "w_b": w(ks[4], (DEPTH, R_V, D_MODEL), R_V),
        "w_o": w(ks[5], (DEPTH, D_MODEL, D_MODEL), D_MODEL),
        "ffn_norm": gain(ks[6], (DEPTH, D_MODEL)),
        "w_up": w(ks[7], (DEPTH, D_MODEL, D_FF), D_MODEL),
        "w_down": w(ks[8], (DEPTH, D_FF, D_MODEL), D_FF),
        "final_norm": gain(ks[9], (D_MODEL,)),
    }

def reference(x, mix_norm, w_in, w_a, w_b, w_o, ffn_norm, w_up, w_down, final_norm):
    for layer in range(DEPTH):
        x = hybrid_layer(x, mix_norm[layer], w_in[layer], w_a[layer], w_b[layer], w_o[layer],
                         ffn_norm[layer], w_up[layer], w_down[layer])
    return rmsnorm(x, final_norm)


_drawn_inputs = setup_inputs


def setup_inputs(seed=0):
    import zlib

    import numpy as np

    out = dict(_drawn_inputs(seed))
    spreads = {}
    factors = {}
    for name, (base, spread) in spreads.items():
        noise = np.random.default_rng([zlib.crc32(name.encode()), seed]).standard_normal(out[name].shape)
        drawn = base * np.exp(spread * noise) if base else spread * noise
        out[name] = __import__('jax').numpy.asarray(drawn.astype(out[name].dtype))
    for name, factor in factors.items():
        out[name] = (out[name] * factor).astype(out[name].dtype)
    return out
```

```python
from contextlib import ExitStack

import concourse.bass as bass
from concourse import mybir

P = 128
F32 = mybir.dt.float32
F32R = mybir.dt.float32r
BF16 = mybir.dt.bfloat16
ALU = mybir.AluOpType
ACT = mybir.ActivationFunctionType

EPS = 1e-6
SHUFFLE = [(i + 8 if i < 8 else i - 8) if i < 16 else i for i in range(32)]

UNIT_CREDIT = 2
MM_CREDIT = 4
BANK_CREDIT = 1


def trunk(nc, a):
    S = a["x"].shape[1]
    D = a["x"].shape[2]
    DEPTH = a["w_in"].shape[0]
    KT = D // P
    TB = S // P
    FF = a["w_up"].shape[2]
    GROUPS, PAIRS = 3, 4
    DH = 64
    A_W = GROUPS * PAIRS * P
    RH, RV = 4, 256
    AW = PAIRS * P
    KA = AW // P
    CH = FF // D
    COL_QR = 3 * A_W
    COL_VR = COL_QR + 2 * RH * P
    COL_GR = COL_VR + RH * RV
    COL_GA = COL_GR + RH * RV
    COL_GB = COL_GA + D

    V_U, P_U, G_U, O_U, M_U = 2, 6, 4, 2, 8
    V0 = 0
    P0 = V0 + GROUPS * V_U
    G0 = P0 + PAIRS * P_U
    O0 = G0 + 4 * G_U
    M0 = O0 + 2 * O_U
    LU = M0 + CH * M_U
    LQ = LU - P0

    with ExitStack() as ctx:
        def sb(name, shape, dt):
            return ctx.enter_context(nc.sbuf_tensor(name, shape, dt))

        def ps(name, cols):
            return ctx.enter_context(nc.psum_tensor(name, [P, cols], F32))

        def sem(name):
            return ctx.enter_context(nc.semaphore(name))

        x = sb("x", [P, KT, S], F32)
        h_hi = sb("h_hi", [P, KT, S], F32R)
        h_lo = sb("h_lo", [P, KT, S], F32R)
        raw = [sb(f"w_raw{i}", [P, 2048], F32) for i in range(2)]
        w_hi = [sb(f"w_hi{i}", [P, 2048], F32R) for i in range(2)]
        w_lo = [sb(f"w_lo{i}", [P, 2048], F32R) for i in range(2)]
        cosA, sinA = sb("cosA", [P, S], F32), sb("sinA", [P, S], F32)
        cosR, sinR = sb("cosR", [P, S], F32), sb("sinR", [P, S], F32)
        decay = sb("decay", [P, S], F32)
        mask = sb("mask", [P, TB, S + 2 * P], BF16)
        ident = sb("ident", [P, P], F32)
        ones_d = sb("ones_d", [P, P], F32)
        ones_r = sb("ones_r", [P, P], F32)
        gains = sb("gains", [P, 2 * DEPTH + 1, KT], F32)
        gain = sb("gain", [P, 2, KT], F32)
        eps = sb("eps", [P, 1], F32)
        tick = sb("tick", [P, 1], F32)

        zone0 = -(-nc.sbuf_base // 64) * 64
        top = {}

        def at(scope, name, shape, dt):
            off = top.get(scope, zone0)
            n = 2 if dt == BF16 else 4
            for d in shape[1:]:
                n *= d
            top[scope] = off + -(-n // 32) * 32
            return nc.alloc_sbuf_tensor_at(name, shape, dt, offset=off)

        z = at("P", "z", [P, KT, S], F32)
        yA = at("P", "yA", [P, KA, S], F32)
        vA = at("P", "vA", [P, TB, A_W], F32)
        qk = at("P", "qk", [P, 2 * GROUPS, S], F32)
        qkR = at("P", "qkR", [P, 2, S], F32)
        vR = at("P", "vR", [P, TB, RV], F32)
        ST = at("P", "ST", [P, sum(range(1, TB + 1)) * P], F32)
        prob = [at("P", f"prob{i}", [P, S + 2 * P], F32) for i in range(1)]
        probT = at("P", "probT", [P, S + 2 * P], F32)
        ysb = at("P", "ysb", [P, TB, P], F32)
        rot = [at("P", f"rot{i}", [P, S], F32) for i in range(1)]
        swp = at("P", "swp", [P, S], F32)
        rcos = at("P", "rcos", [P, S], F32)
        silu = at("P", "silu", [P, 2, S], F32)
        nmax = at("P", "nmax", [P, 2], F32)
        den = at("P", "den", [P, 8], F32)
        rden = at("P", "rden", [P, 8], F32)
        m_hi = at("G", "m_hi", [P, KT, S], F32R)
        m_lo = at("G", "m_lo", [P, KT, S], F32R)
        z_hi = at("G", "z_hi", [P, KT, S], F32R)
        z_lo = at("G", "z_lo", [P, KT, S], F32R)
        pad = top["G"]
        y_hi = at("G", "y_hi", [P, KA, S], F32R)
        y_lo = at("G", "y_lo", [P, KA, S], F32R)
        sA = at("G", "sA", [P, 2, S], F32)
        sB = at("G", "sB", [P, 2, S], F32)
        u_hi, u_lo = z_hi, z_lo
        top["N"] = pad
        ssum = at("N", "ssum", [P, S], F32)
        sq = at("N", "sq", [P, 2, S], F32)
        std = at("N", "std", [P, S], F32)
        hn = at("N", "hn", [P, 2, S], F32)
        relu = at("N", "relu", [P, 2, S], F32)
        relu2 = at("N", "relu2", [P, 2, S], F32)
        x_nat = at("X", "x_nat", [P, TB, D], F32)
        mask_in = at("X", "mask_in", [P, TB, S + 2 * P], F32)
        stage = at("Y", "stage", [P, 2, D], F32)
        for k_, v_ in top.items():
            assert v_ <= nc.sbuf_usable_end, (k_, v_, nc.sbuf_usable_end)

        pj = [ps(f"pj{i}", S) for i in range(2)]
        sc = ps("sc", 2 * S)
        pt = ps("pt", 2 * S)
        yo = ps("yo", S)
        rb = ps("rb", S)
        vbank = [sc[:, 0:S], sc[:, S:2 * S], pt[:, 0:S], pt[:, S:2 * S]]

        const_in = sem("const_in")
        const_set = sem("const_set")
        mask_set = sem("mask_set")
        x_in = sem("x_in")
        x_turned = sem("x_turned")
        x_init = sem("x_init")
        gain_set = sem("gain_set")
        landed = [sem(f"landed{i}") for i in range(2)]
        hi_done = sem("hi_done")
        lo_done = sem("lo_done")
        mm_done = sem("mm_done")
        bank_free = [sem(f"bank_free{i}") for i in range(2)]
        sq_done = sem("sq_done")
        sum_done = sem("sum_done")
        mean_done = sem("mean_done")
        std_done = sem("std_done")
        rstd_done = sem("rstd_done")
        hn_done = sem("hn_done")
        h_hi_done = sem("h_hi_done")
        h_ready = sem("h_ready")
        v_done = sem("v_done")
        v_out = sem("v_out")
        rot_swap = sem("rot_swap")
        rot_sin = sem("rot_sin")
        rot_cos = sem("rot_cos")
        rot_out = sem("rot_out")
        att_qk = sem("att_qk")
        att_masked = sem("att_masked")
        att_exp = sem("att_exp")
        att_turned = sem("att_turned")
        att_probT = sem("att_probT")
        att_pv = sem("att_pv")
        att_rden = sem("att_rden")
        att_y = sem("att_y")
        y_turned = sem("y_turned")
        y_out = sem("y_out")
        decay_in = sem("decay_in")
        st_mm = sem("st_mm")
        st_out = sem("st_out")
        ret_mm = sem("ret_mm")
        ret_sq = sem("ret_sq")
        ret_out = sem("ret_out")
        ret_sum = sem("ret_sum")
        ret_mean = sem("ret_mean")
        ret_std = sem("ret_std")
        ret_rstd = sem("ret_rstd")
        ret_scaled = sem("ret_scaled")
        z_done = sem("z_done")
        sig_exp = sem("sig_exp")
        sig_add = sem("sig_add")
        sig_rec = sem("sig_rec")
        split_hi = sem("split_hi")
        split_done = sem("split_done")
        merged = sem("merged")
        m_hi_done = sem("m_hi_done")
        m_ready = sem("m_ready")
        relu2_done = sem("relu2_done")
        u_hi_done = sem("u_hi_done")
        u_ready = sem("u_ready")
        f_done = sem("f_done")
        f_turned = sem("f_turned")
        f_staged = sem("f_staged")
        out_done = [sem(f"out_done{i}") for i in range(2)]

        st0 = [sum(S - P * i for i in range(j)) for j in range(TB)]

        def by_residue(v):
            return v.rearrange("p (m r) -> p r m", r=4)

        block = ctx.enter_context(nc.Block())

        w_in_t = a["w_in"].rearrange("l (k p) (t c) -> l p k t c", p=P, c=P)
        w_in_u = a["w_in"].rearrange("l (k p) (t c) -> l p k t c", p=P, c=2 * P)
        w_in_v = a["w_in"].rearrange("l (k p) (t c) -> l p k t c", p=P, c=4 * P)
        w_a_u = a["w_a"].rearrange("l (k p) (t c) -> l p k t c", p=P, c=2 * P)
        w_b_u = a["w_b"].rearrange("l (k p) (t c) -> l p k t c", p=P, c=2 * P)
        w_o_u = a["w_o"].rearrange("l (k p) (t c) -> l p k t c", p=P, c=2 * P)
        w_up_u = a["w_up"].rearrange("l (k p) (t c) -> l p k t c", p=P, c=2 * P)
        w_down_u = a["w_down"].rearrange("l (f k p) (t c) -> l p f k t c", p=P, k=KT, c=2 * P)

        @block.sync
        def _(sp):
            sp.dma_start(x_nat[:], a["x"].rearrange("b (t p) d -> p (b t) d", p=P)).then_inc(x_in, 16)
            for dst, name in ((ident, "ident"), (cosA, "cosA"), (sinA, "sinA"), (cosR, "cosR"), (sinR, "sinR"),
                              (mask_in, "mask"), (gains, "gains")):
                sp.dma_start(dst[:], a[name]).then_inc(const_in, 16)

            def load(n, s, halves):
                sp.wait_ge(lo_done, n - 2 + 1 + UNIT_CREDIT)
                for dst, src in halves:
                    sp.dma_start(dst, src).then_inc(landed[s], 16)

            def tiles(s, v, t0, t1):
                d = raw[s][:].rearrange("p (k o c) -> p k o c", o=2, c=P)
                return [(d[:, :, 0, :], v[:, :, t0, :]), (d[:, :, 1, :], v[:, :, t1, :])]

            def cols(s, v, t, kt=KT):
                d = raw[s][:].rearrange("p (k c) -> p k c", k=KT)
                m = kt // 2
                return [(d[:, 0:m, :], v[:, 0:m, t, :]), (d[:, m:kt, :], v[:, m:kt, t, :])]

            with sp.Fori(0, DEPTH) as l:
                with sp.Fori(0, GROUPS) as g:
                    for u in range(V_U):
                        d = raw[u][:].rearrange("p (k c) -> p k c", k=4)
                        load(l * LU + V0 + g * V_U + u, u,
                             [(d[:, m:m + 2, :], w_in_v[l, :, 4 * u + m:4 * u + m + 2, 2 * GROUPS + g, :])
                              for m in (0, 2)])
                with sp.Fori(0, PAIRS) as i:
                    n = l * LU + P0 + i * P_U
                    for g in range(GROUPS):
                        load(n + g, g % 2, tiles(g % 2, w_in_t[l], PAIRS * g + i, PAIRS * (GROUPS + g) + i))
                    load(n + 3, 1, tiles(1, w_in_t[l], COL_QR // P + i, COL_QR // P + RH + i))
                    load(n + 4, 0, cols(0, w_in_u[l], COL_VR // 256 + i))
                    sp.wait_ge(st_out, (l * PAIRS + i) * TB + 1)
                    sp.dma_start(decay[:], a["decay"][i]).then_inc(decay_in, 16)
                    load(n + 5, 1, cols(1, w_in_u[l], COL_GR // 256 + i))
                with sp.Fori(0, 4) as p:
                    n = l * LU + G0 + p * G_U
                    load(n + 0, 0, cols(0, w_in_u[l], COL_GA // 256 + p))
                    load(n + 1, 1, cols(1, w_in_u[l], COL_GB // 256 + p))
                    load(n + 2, 0, cols(0, w_b_u[l], p))
                    load(n + 3, 1, cols(1, w_a_u[l], p, KA))
                with sp.Fori(0, 2) as i:
                    for u in range(O_U):
                        load(l * LU + O0 + i * O_U + u, u, cols(u, w_o_u[l], 2 * i + u))
                with sp.Fori(0, CH) as c:
                    n = l * LU + M0 + c * M_U
                    for u in range(4):
                        load(n + u, u % 2, cols(u % 2, w_up_u[l], 4 * c + u))
                    for u in range(4):
                        load(n + 4 + u, u % 2, cols(u % 2, w_down_u[l, :, c], u))
            sp.wait_ge(lo_done, DEPTH * LU - 1 + UNIT_CREDIT)
            sp.sem_inc(landed[0], 32)

            out_v = a["out"].rearrange("b (t p) d -> (b t) p d", p=P)
            for b in range(TB):
                sp.wait_ge(f_staged, b + 1)
                sp.dma_start(out_v[b], stage[:, b % 2, :]).then_inc(out_done[b % 2], 16)
            for s in out_done:
                sp.wait_ge(s, 16 * TB // 2)

        @block.scalar
        def _(act):
            act.wait_ge(const_set, 3)

            def split_unit(half, n, s):
                act.wait_ge(landed[s], half * 32 + 32)
                act.wait_ge(mm_done, n * 2 - 2 + MM_CREDIT)
                nc.scalar.copy(w_hi[s][:], raw[s][:]).then_inc(hi_done, 1)

            def ahead(l, base, per, i, u):
                k = u + 1
                split_unit(l * (LU // 2) + base // 2 + i * (per // 2) + k // 2, l * LU + base + i * per + k, k % 2)

            def banks(l, base, per, i, u):
                return l * LQ + base - P0 + i * per + u

            def norm(J, after):
                act.wait_ge(x_init, KT)
                for o in range(2):
                    act.wait_ge(bank_free[o], after + BANK_CREDIT)
                for k in range(KT):
                    if k >= 2:
                        act.wait_ge(sum_done, J * (KT - 1) + max(k - 2, 1))
                    nc.scalar.activation(sq[:, k % 2, :], x[:, k, :], ACT.Square).then_inc(sq_done, 1)
                act.wait_ge(mean_done, J + 1)
                nc.scalar.activation(std[:], rb[:], ACT.Sqrt, bias=eps[:]).then_inc(std_done, 1)

            def norm_hi(J):
                for k in range(KT):
                    act.wait_ge(hn_done, J * KT + k + 1)
                    nc.scalar.copy(h_hi[:, k, :], hn[:, k % 2, :]).then_inc(h_hi_done, 1)

            act.wait_ge(landed[0], 32)
            nc.scalar.copy(w_hi[0][:], raw[0][:]).then_inc(hi_done, 1)

            with act.Fori(0, DEPTH) as l:
                norm(2 * l, l * LQ)
                norm_hi(2 * l)
                with act.Fori(0, GROUPS) as g:
                    for u in range(V_U):
                        ahead(l, V0, V_U, g, u)
                with act.Fori(0, PAIRS) as i:
                    J = l * PAIRS + i
                    n = l * LU + P0 + i * P_U
                    q = banks(l, P0, P_U, i, 0)

                    def tile(u, o):
                        act.wait_ge(mm_done, (n + u) * 2 + o + 1 + MM_CREDIT)

                    def rot_in(u, o):
                        t = 2 * u + o
                        tile(u, o)
                        act.wait_ge(rot_out, J * 8 + t + 1)
                        if u < GROUPS:
                            nc.scalar.copy(rot[0][:], pj[o][:]).then_inc(bank_free[o], 1)
                        else:
                            nc.scalar.copy(rot[0][:], pj[o][:])
                            nc.scalar.copy(swp[0:64, :], pj[o][64:128, :])
                            nc.scalar.copy(swp[64:128, :], pj[o][0:64, :]).then_inc(bank_free[o], 1)

                    def exp(b):
                        act.wait_ge(att_masked, J * 8 + b + 1)
                        nc.scalar.activation(prob[0][:], prob[0][:], ACT.Exp, scale=-1.0,
                                             bias=nmax[:, b % 2:b % 2 + 1],
                                             accum_out=den[:, b:b + 1]).then_inc(att_exp, 1)

                    def probT_out(b):
                        act.wait_ge(att_turned, J * 8 + b + 1)
                        if b >= 1:
                            act.wait_ge(att_pv, J * 8 + b)
                        nc.scalar.copy(probT[:], pt[:, 0:S + 2 * P]).then_inc(att_probT, 1)

                    for u in range(GROUPS):
                        ahead(l, P0, P_U, i, u)
                        rot_in(u, 0)
                        rot_in(u, 1)
                    ahead(l, P0, P_U, i, 3)
                    exp(0)
                    rot_in(3, 0)
                    probT_out(0)
                    exp(1)
                    probT_out(1)
                    exp(2)
                    ahead(l, P0, P_U, i, 4)
                    rot_in(3, 1)
                    probT_out(2)
                    exp(3)
                    probT_out(3)
                    exp(4)

                    def vR_out(o):
                        tile(4, o)
                        if o == 0:
                            act.wait_ge(ret_mm, J * 2 + 1 + 1)
                        nc.scalar.copy(vR[:, 2 * o:2 * o + 2, :].rearrange("p b c -> p (b c)"),
                                       pj[o][:]).then_inc(bank_free[o], 1)

                    vR_out(0)
                    probT_out(4)
                    exp(5)
                    probT_out(5)
                    exp(6)
                    ahead(l, P0, P_U, i, 5)
                    vR_out(1)
                    probT_out(6)
                    exp(7)
                    probT_out(7)

                    def ret_square(e):
                        act.wait_ge(ret_out, J * 2 + e + 1)
                        nc.scalar.activation(sqR[e], rb[:],
                                             ACT.Square).then_inc(ret_sq, 1)

                    def gate_exp(o):
                        tile(5, o)
                        nc.scalar.activation(silu[:, o, :], pj[o][:], ACT.Exp, scale=-1.0).then_inc(sig_exp, 1)

                    sqR = [probT[:, 0:S], rot[0][:]]
                    act.wait_ge(att_pv, J * 8 + 8)
                    ret_square(0)
                    gate_exp(0)
                    ret_square(1)
                    gate_exp(1)
                    act.wait_ge(ret_mean, J + 1)
                    nc.scalar.activation(swp[:], rb[:], ACT.Sqrt, bias=eps[:]).then_inc(ret_std, 1)
                ahead(l, G0, G_U, 0, 0)
                act.wait_ge(z_done, l * KT + KT)
                act.wait_ge(y_out, l * PAIRS + PAIRS + 1)
                for k in range(KT):
                    nc.scalar.copy(z_hi[:, k, :], z[:, k, :]).then_inc(split_hi, 1)
                for k in range(KA):
                    nc.scalar.copy(y_hi[:, k, :], yA[:, k, :]).then_inc(split_hi, 1)
                with act.Fori(0, 4) as p:
                    J = l * 4 + p
                    n = l * LU + G0 + p * G_U
                    for u, dst in ((0, sA), (1, sB)):
                        for o in range(2):
                            act.wait_ge(mm_done, (n + u) * 2 + o + 1 + MM_CREDIT)
                            act.wait_ge(m_ready, J * 2 + o + 1)
                            nc.scalar.activation(dst[:, o, :], pj[o][:], ACT.Sigmoid).then_inc(bank_free[o], 1)
                        ahead(l, G0, G_U, p, u + 1)
                    ahead(l, G0, G_U, p, 3)
                    ahead(l, G0, G_U, p, 4)
                for u in range(1, 2 * O_U):
                    ahead(l, O0, O_U, 0, u)
                norm(2 * l + 1, l * LQ + M0 - P0)
                norm_hi(2 * l + 1)
                with act.Fori(0, CH) as c:
                    J = l * CH + c
                    n = l * LU + M0 + c * M_U
                    for u in range(4):
                        ahead(l, M0, M_U, c, u)
                        for o in range(2):
                            t = 2 * u + o
                            act.wait_ge(mm_done, (n + u) * 2 + o + 1 + MM_CREDIT)
                            nc.scalar.activation(relu[:, o, :], pj[o][:], ACT.Relu).then_inc(bank_free[o], 1)
                            act.wait_ge(relu2_done, J * 8 + t + 1)
                            nc.scalar.copy(u_hi[:, t, :], relu2[:, o, :]).then_inc(u_hi_done, 1)
                    for u in range(4, 8):
                        ahead(l, M0, M_U, c, u)
            norm(2 * DEPTH, DEPTH * LQ)
            for b in range(TB):
                act.wait_ge(f_turned, b + 1)
                if b >= 2:
                    act.wait_ge(out_done[b % 2], 16 * (b // 2))
                nc.scalar.copy(stage[:, b % 2, :], (sc, pt)[b % 2][:]).then_inc(f_staged, 1)

        @block.gpsimd
        def _(pool):
            nc.gpsimd.memset(ones_d[:], 1.0 / D).then_inc(const_set, 1)
            nc.gpsimd.memset(ones_r[:], 1.0 / RV).then_inc(const_set, 1)
            nc.gpsimd.memset(eps[:], EPS).then_inc(const_set, 1)
            pool.sem_inc(lo_done, UNIT_CREDIT)

            def lo(n, s):
                pool.wait_ge(hi_done, n + 1)
                nc.gpsimd.tensor_tensor(w_lo[s][:], raw[s][:], w_hi[s][:], ALU.subtract).then_inc(lo_done, 1)

            lo(0, 0)
            pool.wait_ge(const_in, 16 * 7)
            with pool.Fori(0, DEPTH) as l:
                with pool.Fori(0, GROUPS) as g:
                    for u in range(V_U):
                        lo(l * LU + V0 + g * V_U + u + 1, (u + 1) % 2)
                with pool.Fori(0, PAIRS) as i:
                    J = l * PAIRS + i
                    n = l * LU + P0 + i * P_U
                    q = l * LQ + i * P_U
                    for u in range(P_U):
                        lo(n + u + 1, (u + 1) % 2)
                        for o in range(2 if u < 4 else 0):
                            pool.wait_ge(bank_free[o], q + u + 1 + BANK_CREDIT)
                            pool.wait_ge(rot_out, J * 8 + 2 * u + o + 1)
                            nc.gpsimd.tensor_tensor(rcos[:], rot[0][:], (cosA if u < 3 else cosR)[:],
                                                    ALU.mult).then_inc(rot_cos, 1)
                with pool.Fori(0, (LU - G0) // 2) as j:
                    for u in range(2):
                        lo(l * LU + G0 + 2 * j + u + 1, (u + 1) % 2)

        @block.vector
        def _(dve):
            for s in bank_free:
                dve.sem_inc(s, BANK_CREDIT)
            dve.sem_inc(rot_out, 1)
            dve.sem_inc(y_out, 1)
            dve.sem_inc(ret_std, 1)
            dve.sem_inc(st_out, 1)
            dve.sem_inc(v_out, TB)
            dve.sem_inc(m_ready, 2)
            dve.wait_ge(const_in, 16 * 7)

            nc.vector.tensor_copy(mask[:], mask_in[:]).then_inc(mask_set, 1)
            for k in range(KT):
                dve.wait_ge(x_turned, k + 1)
                nc.vector.tensor_copy(x[:, k, :], pj[k % 2][:]).then_inc(x_init, 1)

            def norm(J):
                for k in range(1, KT):
                    dve.wait_ge(sq_done, J * KT + k + 1)
                    if k > 1:
                        dve.wait_ge(sum_done, J * (KT - 1) + k - 1)
                    nc.vector.tensor_tensor(ssum[:], sq[:, 0, :] if k == 1 else ssum[:], sq[:, k % 2, :],
                                            ALU.add).then_inc(sum_done, 1)
                dve.wait_ge(std_done, J + 1)
                nc.vector.reciprocal(std[:], std[:]).then_inc(rstd_done, 1)
                dve.wait_ge(rstd_done, J + 1)

            def norm_h(J, which):
                def scaled(k):
                    if k >= 2:
                        dve.wait_ge(h_ready, J * KT + k - 1)
                    nc.vector.scalar_tensor_tensor(out=hn[:, k % 2, :], in0=x[:, k, :],
                                                   scalar=gain[:, which, k:k + 1], in1=std[:],
                                                   op0=ALU.mult, op1=ALU.mult).then_inc(hn_done, 1)

                scaled(0)
                for k in range(KT):
                    if k + 1 < KT:
                        scaled(k + 1)
                    dve.wait_ge(h_hi_done, J * KT + k + 1)
                    nc.vector.tensor_tensor(h_lo[:, k, :], hn[:, k % 2, :], h_hi[:, k, :],
                                            ALU.subtract).then_inc(h_ready, 1)

            with dve.Fori(0, DEPTH) as l:
                nc.vector.tensor_scalar(gain[:].rearrange("p w k -> p (w k)"),
                                        gains[:, bass.ds(l * 2, 2), :].rearrange("p w k -> p (w k)"), 1.0, None,
                                        ALU.mult).then_inc(gain_set, 1)
                norm(2 * l)
                dve.wait_ge(gain_set, l + 1)
                norm_h(2 * l, 0)
                with dve.Fori(0, GROUPS) as g:
                    J = l * GROUPS + g
                    for b in range(TB):
                        if b < TB - 1:
                            dve.wait_ge(v_done, J * (TB - 1) + b + 1)
                        else:
                            dve.wait_ge(mm_done, (l * LU + V0 + g * V_U + 2) * 2 + MM_CREDIT)
                        nc.vector.tensor_scalar(vA[:, b, bass.ds(g * 512, 512)], vbank[b], 1.0, None,
                                                ALU.mult).then_inc(v_out, 1)
                with dve.Fori(0, PAIRS) as i:
                    J = l * PAIRS + i
                    n = l * LU + P0 + i * P_U
                    q = l * LQ + i * P_U

                    def rotary(u, o):
                        t = 2 * u + o
                        dve.wait_ge(bank_free[o], q + u + 1 + BANK_CREDIT)
                        if u < GROUPS:
                            nc.vector.memset(tick[:], 0.0)
                            nc.vector.stream_shuffle(swp[:], rot[0][:], SHUFFLE).then_inc(rot_swap, 1)
                            dve.wait_ge(rot_swap, J * 6 + t + 1)
                        nc.vector.tensor_tensor(swp[:], swp[:], (sinA if u < GROUPS else sinR)[:],
                                                ALU.mult).then_inc(rot_sin, 1)
                        dve.wait_ge(rot_sin, J * 8 + t + 1)
                        dve.wait_ge(rot_cos, J * 8 + t + 1)
                        if u < GROUPS:
                            nc.vector.tensor_tensor(qk[:, t, :].rearrange("p (r m) -> p r m", r=4),
                                                    by_residue(rcos[:]), by_residue(swp[:]),
                                                    ALU.add).then_inc(rot_out, 1)
                        else:
                            nc.vector.tensor_tensor(qkR[:, o, :], rcos[:], swp[:], ALU.add).then_inc(rot_out, 1)

                    def masked(b):
                        if b == 0:
                            dve.wait_ge(mask_set, 1)
                        dve.wait_ge(att_qk, J * 8 + b + 1)
                        if b >= 1:
                            dve.wait_ge(att_turned, J * 8 + b)
                        nc.vector.memset(tick[:], 0.0)
                        nc.vector.tensor_tensor_reduce(
                            out=prob[0][:], in0=sc[:, 0:S + 2 * P], in1=mask[:, b // 2, :],
                            scale=-(DH ** -0.5), scalar=3e38, op0=ALU.add, op1=ALU.min,
                            accum_out=nmax[:, b % 2:b % 2 + 1]).then_inc(att_masked, 1)

                    def y_block(b):
                        dve.wait_ge(att_exp, J * 8 + b + 1)
                        nc.vector.reciprocal(rden[:, b:b + 1], den[:, b:b + 1]).then_inc(att_rden, 1)
                        dve.wait_ge(att_pv, J * 8 + b + 1)
                        dve.wait_ge(att_rden, J * 8 + b + 1)
                        c = (b % 2) * DH
                        nc.vector.tensor_scalar(ysb[:, b // 2, c:c + DH],
                                                yo[:, (b // 2) * P + c:(b // 2) * P + c + DH],
                                                rden[:, b:b + 1], None, ALU.mult).then_inc(att_y, 1)

                    def st_decayed(j):
                        dve.wait_ge(st_mm, J * TB + j + 1)
                        w = S - j * P
                        if j == 0:
                            dve.wait_ge(decay_in, J * 16 + 16)
                        nc.vector.tensor_tensor(ST[:, st0[j]:st0[j] + w], rb[:, 0:w], decay[:, 0:w],
                                                ALU.mult).then_inc(st_out, 1)

                    def ret_copy(e):
                        dve.wait_ge(ret_mm, J * 2 + e + 1 + 2)
                        nc.vector.tensor_scalar(z[:, bass.ds(2 * i + e, 1), :].rearrange("p k s -> p (k s)"),
                                                rb[:], 1.0, None, ALU.mult).then_inc(ret_out, 1)

                    def silu_gate(o):
                        dve.wait_ge(sig_exp, J * 2 + o + 1)
                        nc.vector.tensor_scalar(silu[:, o, :], silu[:, o, :], 1.0, None, ALU.add).then_inc(sig_add, 1)
                        dve.wait_ge(sig_add, J * 2 + o + 1)
                        nc.vector.reciprocal(silu[:, o, :], silu[:, o, :]).then_inc(sig_rec, 1)
                        dve.wait_ge(sig_rec, J * 2 + o + 1)
                        nc.vector.tensor_tensor(silu[:, o, :], pj[o][:], silu[:, o, :],
                                                ALU.mult).then_inc(bank_free[o], 1)

                    for t in range(6):
                        rotary(t // 2, t % 2)
                    masked(0)
                    rotary(3, 0)
                    masked(1)
                    y_block(0)
                    masked(2)
                    y_block(1)
                    masked(3)
                    rotary(3, 1)
                    for s in range(4):
                        y_block(2 + s)
                        masked(4 + s)
                        st_decayed(s)
                    y_block(6)
                    ret_copy(0)
                    y_block(7)
                    silu_gate(0)
                    ret_copy(1)
                    dve.wait_ge(ret_sq, J * 2 + 2)
                    nc.vector.tensor_tensor(rcos[:], probT[:, 0:S], rot[0][:], ALU.add).then_inc(ret_sum, 1)
                    silu_gate(1)
                    dve.wait_ge(y_turned, J + 1)
                    nc.vector.tensor_scalar(
                        yA[:, bass.ds(i, 1), :].rearrange("p k (m r) -> p (k m) r", r=4),
                        yo[:].rearrange("p (r m) -> p m r", r=4), 1.0, None, ALU.mult).then_inc(y_out, 1)
                    dve.wait_ge(ret_std, J + 1 + 1)
                    nc.vector.reciprocal(swp[:], swp[:]).then_inc(ret_rstd, 1)
                    dve.wait_ge(ret_rstd, J + 1)
                    for e in range(2):
                        ze = z[:, bass.ds(2 * i + e, 1), :].rearrange("p k s -> p (k s)")
                        nc.vector.tensor_tensor(silu[:, e, :], silu[:, e, :], swp[:],
                                                ALU.mult).then_inc(ret_scaled, 1)
                        dve.wait_ge(ret_scaled, J * 2 + e + 1)
                        nc.vector.tensor_tensor(ze, ze, silu[:, e, :], ALU.mult).then_inc(z_done, 1)
                for k in range(KT):
                    dve.wait_ge(split_hi, l * (KT + KA) + k + 1)
                    nc.vector.tensor_tensor(z_lo[:, k, :], z[:, k, :], z_hi[:, k, :],
                                            ALU.subtract).then_inc(split_done, 1)
                for k in range(KA):
                    dve.wait_ge(split_hi, l * (KT + KA) + KT + k + 1)
                    nc.vector.tensor_tensor(y_lo[:, k, :], yA[:, k, :], y_hi[:, k, :],
                                            ALU.subtract).then_inc(split_done, 1)
                with dve.Fori(0, 4) as p:
                    J = l * 4 + p
                    n = l * LU + G0 + p * G_U
                    q = l * LQ + G0 - P0 + p * G_U
                    for u, dst in ((2, sB), (3, sA)):
                        for o in range(2):
                            dve.wait_ge(mm_done, (n + u) * 2 + o + 1 + MM_CREDIT)
                            nc.vector.tensor_tensor(dst[:, o, :], pj[o][:], dst[:, o, :],
                                                    ALU.mult).then_inc(bank_free[o], 1)
                    for o in range(2):
                        dve.wait_ge(bank_free[o], q + 4 + BANK_CREDIT)
                        nc.vector.tensor_tensor(sA[:, o, :], sA[:, o, :], sB[:, o, :], ALU.add).then_inc(merged, 1)
                    for o in range(2):
                        mh = m_hi[:, bass.ds(2 * p + o, 1), :].rearrange("p k s -> p (k s)")
                        ml = m_lo[:, bass.ds(2 * p + o, 1), :].rearrange("p k s -> p (k s)")
                        dve.wait_ge(merged, J * 2 + o + 1)
                        nc.vector.tensor_scalar(mh, sA[:, o, :], 1.0, None, ALU.mult).then_inc(m_hi_done, 1)
                        dve.wait_ge(m_hi_done, J * 2 + o + 1)
                        nc.vector.tensor_tensor(ml, sA[:, o, :], mh, ALU.subtract).then_inc(m_ready, 1)
                with dve.Fori(0, 2) as i:
                    n = l * LU + O0 + i * O_U
                    for u in range(O_U):
                        for o in range(2):
                            dve.wait_ge(mm_done, (n + u) * 2 + o + 1 + MM_CREDIT)
                            xk = x[:, bass.ds(4 * i + 2 * u + o, 1), :].rearrange("p k s -> p (k s)")
                            nc.vector.tensor_tensor(xk, pj[o][:], xk, ALU.add).then_inc(bank_free[o], 1)
                norm(2 * l + 1)
                norm_h(2 * l + 1, 1)
                with dve.Fori(0, CH) as c:
                    J = l * CH + c
                    n = l * LU + M0 + c * M_U
                    q = l * LQ + M0 - P0 + c * M_U
                    for u in range(4):
                        for o in range(2):
                            t = 2 * u + o
                            dve.wait_ge(bank_free[o], q + u + 1 + BANK_CREDIT)
                            nc.vector.tensor_tensor(relu2[:, o, :], relu[:, o, :], relu[:, o, :],
                                                    ALU.mult).then_inc(relu2_done, 1)
                            dve.wait_ge(u_hi_done, J * 8 + t + 1)
                            nc.vector.tensor_tensor(u_lo[:, t, :], relu2[:, o, :], u_hi[:, t, :],
                                                    ALU.subtract).then_inc(u_ready, 1)
                    for u in range(4, 8):
                        for o in range(2):
                            t = 2 * (u - 4) + o
                            dve.wait_ge(mm_done, (n + u) * 2 + o + 1 + MM_CREDIT)
                            nc.vector.tensor_tensor(x[:, t, :], pj[o][:], x[:, t, :],
                                                    ALU.add).then_inc(bank_free[o], 1)
            norm(2 * DEPTH)
            for k in range(KT):
                nc.vector.scalar_tensor_tensor(out=x[:, k, :], in0=x[:, k, :],
                                               scalar=gains[:, 2 * DEPTH, k:k + 1], in1=std[:],
                                               op0=ALU.mult, op1=ALU.mult).then_inc(f_done, 1)

        @block.tensor
        def _(pe):
            pe.sem_inc(mm_done, MM_CREDIT)
            pe.sem_inc(ret_mm, 2)
            pe.wait_ge(const_in, 16 * 7)
            pe.wait_ge(const_set, 3)
            pe.wait_ge(x_in, 16)
            for k in range(KT):
                if k >= 2:
                    pe.wait_ge(x_init, k - 1)
                for b in range(TB):
                    last = nc.tensor.transpose(pj[k % 2][:, b * P:(b + 1) * P], x_nat[:, b, k * P:(k + 1) * P],
                                               ident[:])
                last.then_inc(x_turned, 1)
            pe.wait_ge(x_init, KT)

            def mean(J):
                pe.wait_ge(sum_done, (J + 1) * (KT - 1))
                nc.tensor.matmul(rb[:], ones_d[:], ssum[:], start=True, stop=True).then_inc(mean_done, 1)

            def weights(n):
                pe.wait_ge(lo_done, n + 1 + UNIT_CREDIT)

            def three(out, s, wc, acts, first, last):
                nc.tensor.matmul(out, w_hi[s][:, wc], acts[0], start=first, stop=False)
                nc.tensor.matmul(out, w_hi[s][:, wc], acts[1], start=False, stop=False)
                return nc.tensor.matmul(out, w_lo[s][:, wc], acts[0], start=False, stop=last)

            def tile_half(s, o, acts, ks, kt=KT, ready=None):
                for k in ks:
                    if ready:
                        ready(k)
                    mm = three(pj[o][:], s, slice(k * 256 + o * P, k * 256 + o * P + P),
                               (acts[0][:, k, :], acts[1][:, k, :]), k == 0, k == kt - 1)
                if ks[-1] == kt - 1:
                    mm.then_inc(mm_done, 1)

            def unit(n, q, s, acts, kt=KT, ready=None):
                weights(n)
                for o in range(2):
                    pe.wait_ge(bank_free[o], q + BANK_CREDIT)
                    tile_half(s, o, acts, range(kt), kt, ready if o == 0 else None)

            h = (h_hi, h_lo)
            with pe.Fori(0, DEPTH) as l:
                mean(2 * l)
                with pe.Fori(0, GROUPS) as g:
                    J = l * GROUPS + g
                    for u in range(V_U):
                        weights(l * LU + V0 + g * V_U + u)
                        for kk in range(4):
                            k = 4 * u + kk
                            pe.wait_ge(h_ready, l * 2 * KT + k + 1)
                            w = slice(kk * 512, kk * 512 + 512)
                            for b in range(TB):
                                if k == 0:
                                    pe.wait_ge(v_out, J * TB + b + 1)
                                hh, hl = by_residue(h_hi[:, k, :])[:, b], by_residue(h_lo[:, k, :])[:, b]
                                nc.tensor.matmul(vbank[b], hh, w_hi[u][:, w], start=(k == 0), stop=False)
                                nc.tensor.matmul(vbank[b], hh, w_lo[u][:, w], start=False, stop=False)
                                mm = nc.tensor.matmul(vbank[b], hl, w_hi[u][:, w], start=False, stop=(k == KT - 1))
                                if k == KT - 1 and b < TB - 1:
                                    mm.then_inc(v_done, 1)
                        mm.then_inc(mm_done, 2)
                with pe.Fori(0, PAIRS) as i:
                    J = l * PAIRS + i
                    n = l * LU + P0 + i * P_U
                    q = l * LQ + i * P_U

                    off = [[pe.snap(i * P + (g * AW + hh * DH)) for hh in range(2)] for g in range(GROUPS)]

                    def scores(b):
                        r, rows = b // 2, slice((b % 2) * DH, (b % 2) * DH + DH)
                        if b == 0:
                            pe.wait_ge(rot_out, J * 8 + 6 + 1)
                            pe.wait_ge(v_out, l * GROUPS * TB + (GROUPS + 1) * TB)
                        else:
                            pe.wait_ge(att_masked, J * 8 + b)
                        Q = slice(r * P, r * P + P)
                        nc.tensor.matmul(sc[:, 0:S], qk[rows, 0, Q], qk[rows, 1, :], start=True, stop=True)
                        nc.tensor.matmul(sc[:, S:S + P], qk[rows, 2, Q], qk[rows, 3, Q], start=True, stop=True)
                        nc.tensor.matmul(sc[:, S + P:S + 2 * P], qk[rows, 4, Q], qk[rows, 5, Q],
                                         start=True, stop=True).then_inc(att_qk, 1)

                    def turn(b):
                        pe.wait_ge(att_exp, J * 8 + b + 1)
                        if b >= 1:
                            pe.wait_ge(att_probT, J * 8 + b)
                        for j in range(TB + 2):
                            mm = nc.tensor.transpose(pt[:, j * P:(j + 1) * P], prob[0][:, j * P:(j + 1) * P], ident[:])
                        mm.then_inc(att_turned, 1)

                    def values(b):
                        r, hh = b // 2, b % 2
                        out = yo[:, r * P + hh * DH:r * P + hh * DH + DH]
                        if b == 0:
                            pe.wait_ge(y_out, J + 1)
                        else:
                            pe.wait_ge(att_y, J * 8 + b)
                        pe.wait_ge(att_probT, J * 8 + b + 1)
                        for j in range(TB + 2):
                            blk, g = (j, 0) if j < TB else (r, j - TB + 1)
                            mm = nc.tensor.matmul(out, probT[:, j * P:(j + 1) * P],
                                                  vA[:, blk, bass.ds(off[g][hh], DH)],
                                                  start=(j == 0), stop=(j == TB + 1))
                        mm.then_inc(att_pv, 1)

                    def st(j):
                        if j == 0:
                            pe.wait_ge(rot_out, J * 8 + 8 + 1)
                            pe.wait_ge(ret_std, J + 1)
                        else:
                            pe.wait_ge(st_out, J * TB + j + 1)
                        nc.tensor.matmul(rb[:, 0:S - j * P], qkR[:, 1, j * P:(j + 1) * P], qkR[:, 0, j * P:S],
                                         start=True, stop=True).then_inc(st_mm, 1)

                    def ret(e):
                        if e == 0:
                            pe.wait_ge(st_out, J * TB + TB + 1)
                            for o in range(2):
                                pe.wait_ge(bank_free[o], q + 5 + BANK_CREDIT)
                        else:
                            pe.wait_ge(ret_out, J * 2 + 1)
                            pe.wait_ge(ret_sq, J * 2 + 1)
                        for j in range(TB):
                            w = S - j * P
                            mm = nc.tensor.matmul(rb[:, j * P:S], vR[:, j, e * P:(e + 1) * P],
                                                  ST[:, st0[j]:st0[j] + w], start=(j == 0), stop=(j == TB - 1))
                        mm.then_inc(ret_mm, 1)

                    for u in range(GROUPS):
                        unit(n + u, q + u, u % 2, h)
                    for s in range(12):
                        u, o, half = 3 + s // 4, s // 2 % 2, s % 2
                        sl = u % 2
                        if s % 4 == 0:
                            weights(n + u)
                        if half == 0:
                            pe.wait_ge(bank_free[o], q + u + BANK_CREDIT)
                        if u != 4:
                            tile_half(sl, o, h, range(4 * half, 4 * half + 4))
                        else:
                            b = 2 * o + half
                            out = pj[o][:, half * RV:(half + 1) * RV]
                            for k in range(KT):
                                w = slice(k * 256, k * 256 + 256)
                                hh, hl = h_hi[:, k, b * P:(b + 1) * P], h_lo[:, k, b * P:(b + 1) * P]
                                nc.tensor.matmul(out, hh, w_hi[sl][:, w], start=(k == 0), stop=False)
                                nc.tensor.matmul(out, hh, w_lo[sl][:, w], start=False, stop=False)
                                mm = nc.tensor.matmul(out, hl, w_hi[sl][:, w], start=False, stop=(k == KT - 1))
                            if half == 1:
                                mm.then_inc(mm_done, 1)
                        if 3 <= s < 11:
                            values(s - 3)
                        if 2 <= s < 10:
                            turn(s - 2)
                        if 1 <= s < 9:
                            scores(s - 1)
                        if 5 <= s < 9:
                            st(s - 5)
                        if 9 <= s < 11:
                            ret(s - 9)
                    pe.wait_ge(att_y, J * 8 + 8)
                    for r in range(TB):
                        mm = nc.tensor.transpose(yo[:, r * P:(r + 1) * P], ysb[:, r, :], ident[:])
                    mm.then_inc(y_turned, 1)
                    pe.wait_ge(ret_sum, J + 1)
                    pe.wait_ge(ret_out, J * 2 + 2)
                    nc.tensor.matmul(rb[:], ones_r[:], rcos[:], start=True, stop=True).then_inc(ret_mean, 1)
                with pe.Fori(0, 4) as p:
                    n = l * LU + G0 + p * G_U
                    q = l * LQ + G0 - P0 + p * G_U
                    unit(n, q, 0, h)
                    unit(n + 1, q + 1, 1, h)
                    unit(n + 2, q + 2, 0, (z_hi, z_lo), KT, lambda k: pe.wait_ge(split_done, l * (KT + KA) + k + 1))
                    unit(n + 3, q + 3, 1, (y_hi, y_lo), KA,
                         lambda k: pe.wait_ge(split_done, l * (KT + KA) + KT + k + 1))
                with pe.Fori(0, 2) as i:
                    for u in range(O_U):
                        unit(l * LU + O0 + i * O_U + u, l * LQ + O0 - P0 + i * O_U + u, u, (m_hi, m_lo), KT,
                             (lambda k: pe.wait_ge(m_ready, l * KT + k + 1 + 2)) if u == 0 else None)
                mean(2 * l + 1)
                with pe.Fori(0, CH) as c:
                    n = l * LU + M0 + c * M_U
                    q = l * LQ + M0 - P0 + c * M_U
                    for u in range(4):
                        unit(n + u, q + u, u % 2, h, KT,
                             (lambda k: pe.wait_ge(h_ready, l * 2 * KT + KT + k + 1)) if u == 0 else None)
                    for u in range(4):
                        unit(n + 4 + u, q + 4 + u, u % 2, (u_hi, u_lo), KT,
                             (lambda k: pe.wait_ge(u_ready, (l * CH + c) * 8 + k + 1)) if u == 0 else None)
            mean(2 * DEPTH)
            for b in range(TB):
                if b == 0:
                    pe.wait_ge(f_done, KT)
                if b >= 2:
                    pe.wait_ge(f_staged, b - 1)
                for k in range(KT):
                    mm = nc.tensor.transpose((sc, pt)[b % 2][:, k * P:(k + 1) * P], x[:, k, b * P:(b + 1) * P], ident[:])
                mm.then_inc(f_turned, 1)


def constants(S, D):
    import numpy as np

    f = np.float32
    pos = np.arange(S, dtype=f)

    def tables(half, base):
        inv = (f(1.0) / (f(base) ** (np.arange(half, dtype=f) / f(half)))).astype(f)
        ang = (pos[None, :] * inv[:, None]).astype(f)
        return np.cos(ang).astype(f), np.sin(ang).astype(f)

    cosA, sinA = np.ones((P, S), f), np.zeros((P, S), f)
    c, s = tables(8, 500000.0)
    for h in (0, 64):
        cosA[h:h + 8], cosA[h + 8:h + 16] = c, c
        sinA[h:h + 8], sinA[h + 8:h + 16] = -s, s
    c, s = tables(64, 10000.0)
    cosR, sinR = np.concatenate([c, c]), np.concatenate([-s, s])

    lg = np.log1p(-(f(2.0) ** (f(-5.0) - np.arange(4, dtype=f)))).astype(f)
    diff = (np.arange(S)[None, :] - np.arange(P)[:, None]).astype(f)
    decay = np.exp(np.maximum(diff, f(0))[:, None, :] * lg[None, :, None])
    decay = (np.where(diff[:, None, :] >= 0, decay, f(0)) * f(P ** -0.5)).astype(f)

    token = np.array([4 * m + r for r in range(4) for m in range(S // 4)])
    mask = np.empty((P, 4, S + 2 * P), f)
    for r in range(4):
        tq = token[r * P:(r + 1) * P]
        d1 = tq[:, None] - token[None, :]
        d2 = tq[:, None] - tq[None, :]
        mask[:, r, 0:S] = np.where((d1 >= 0) & (d1 <= 128), 0, -1e30)
        mask[:, r, S:S + P] = np.where(d2 >= 0, 0, -1e30)
        mask[:, r, S + P:] = np.where((d2 >= 0) & (d2 % 16 == 0), 0, -1e30)
    return {"cosA": cosA, "sinA": sinA, "cosR": cosR.astype(f), "sinR": sinR.astype(f), "decay": np.ascontiguousarray(decay.transpose(1, 0, 2)),
            "mask": mask, "ident": np.eye(P, dtype=f)}


_INS = ["x", "w_in", "w_a", "w_b", "w_o", "w_up", "w_down"]


def kernel(**inputs):
    import numpy as np
    import concourse.bacc as bacc
    from concourse.bass_utils import run_bass_kernel_spmd

    nc = bacc.Bacc("TRN2", target_bir_lowering=False, num_devices=1)
    arrays = {n: np.ascontiguousarray(inputs[n]) for n in _INS}
    shape = arrays["x"].shape
    norms = [g for pair in zip(inputs["mix_norm"], inputs["ffn_norm"]) for g in pair] + [inputs["final_norm"]]
    gains = np.stack([np.asarray(g) for g in norms]).reshape(len(norms), -1, P)
    arrays["gains"] = np.ascontiguousarray(gains.transpose(2, 0, 1))
    arrays.update(constants(shape[1], shape[2]))
    feeds, aps = {}, {}
    for name, v in arrays.items():
        feeds[f"in_{name}"] = v
        aps[name] = nc.dram_tensor(f"in_{name}", v.shape, mybir.dt.from_np(v.dtype), kind="ExternalInput").ap()
    aps["out"] = nc.dram_tensor("out_x", shape, F32, kind="ExternalOutput").ap()
    trunk(nc, aps)
    r = run_bass_kernel_spmd(nc, [feeds], core_ids=[0])
    return r.results[0]["out_x"]
```

```python
from contextlib import ExitStack

import concourse.bass as bass
from concourse import mybir

P = 128
F32 = mybir.dt.float32
F32R = mybir.dt.float32r
BF16 = mybir.dt.bfloat16
ALU = mybir.AluOpType
ACT = mybir.ActivationFunctionType

EPS = 1e-6
SHUFFLE = [(i + 8 if i < 8 else i - 8) if i < 16 else i for i in range(32)]

UNIT_CREDIT = 2
MM_CREDIT = 4
BANK_CREDIT = 1


def trunk(nc, a):
    S = a["x"].shape[1]
    D = a["x"].shape[2]
    DEPTH = a["w_in"].shape[0]
    KT = D // P
    TB = S // P
    FF = a["w_up"].shape[2]
    GROUPS, PAIRS = 3, 4
    DH = 64
    A_W = GROUPS * PAIRS * P
    RH, RV = 4, 256
    AW = PAIRS * P
    KA = AW // P
    CH = FF // D
    COL_QR = 3 * A_W
    COL_VR = COL_QR + 2 * RH * P
    COL_GR = COL_VR + RH * RV
    COL_GA = COL_GR + RH * RV
    COL_GB = COL_GA + D

    V_U, P_U, G_U, O_U, M_U = 2, 6, 4, 2, 8
    V0 = 0
    P0 = V0 + GROUPS * V_U
    G0 = P0 + PAIRS * P_U
    O0 = G0 + 4 * G_U
    M0 = O0 + 2 * O_U
    LU = M0 + CH * M_U
    LQ = LU - P0

    with ExitStack() as ctx:
        def sb(name, shape, dt):
            return ctx.enter_context(nc.sbuf_tensor(name, shape, dt))

        def ps(name, cols):
            return ctx.enter_context(nc.psum_tensor(name, [P, cols], F32))

        def sem(name):
            return ctx.enter_context(nc.semaphore(name))

        x = sb("x", [P, KT, S], F32)
        h_hi = sb("h_hi", [P, KT, S], F32R)
        h_lo = sb("h_lo", [P, KT, S], F32R)
        raw = [sb(f"w_raw{i}", [P, 2048], F32) for i in range(2)]
        w_hi = [sb(f"w_hi{i}", [P, 2048], F32R) for i in range(2)]
        w_lo = [sb(f"w_lo{i}", [P, 2048], F32R) for i in range(2)]
        tables = sb("tables", [P, 4, S], F32)
        cosA, sinA, cosR, sinR = (tables[:, i, :] for i in range(4))
        rstd_all = sb("rstd_all", [P, S], F32)
        decay = sb("decay", [P, S], F32)
        mask = sb("mask", [P, TB, S + 2 * P], BF16)
        ident = sb("ident", [P, P], F32)
        ones = sb("ones", [P, P], F32)
        inv_d = sb("inv_d", [P, 1], F32)
        ones_r = sb("ones_r", [P, P], F32)
        gains = sb("gains", [P, 2 * DEPTH + 1, KT], F32)
        gain = sb("gain", [P, 2, KT], F32)
        std = sb("std", [P, 2 * TB], F32)
        rstd = sb("rstd", [P, 2 * TB], F32)
        eps = sb("eps", [P, 1], F32)
        tick = sb("tick", [P, 1], F32)

        zone0 = -(-nc.sbuf_base // 64) * 64
        top = {}

        def at(scope, name, shape, dt):
            off = top.get(scope, zone0)
            n = 2 if dt == BF16 else 4
            for d in shape[1:]:
                n *= d
            top[scope] = off + -(-n // 32) * 32
            return nc.alloc_sbuf_tensor_at(name, shape, dt, offset=off)

        z = at("P", "z", [P, KT, S], F32)
        yA = at("P", "yA", [P, KA, S], F32)
        vA = at("P", "vA", [P, TB, A_W], F32)
        qk = at("P", "qk", [P, 2 * GROUPS, S], F32)
        qkR = at("P", "qkR", [P, 2, S], F32)
        vR = at("P", "vR", [P, TB, RV], F32)
        ST = at("P", "ST", [P, sum(range(1, TB + 1)) * P], F32)
        prob = [at("P", f"prob{i}", [P, S + 2 * P], F32) for i in range(1)]
        probT = at("P", "probT", [P, S + 2 * P], F32)
        ysb = at("P", "ysb", [P, TB, P], F32)
        rot = [at("P", f"rot{i}", [P, S], F32) for i in range(1)]
        swp = at("P", "swp", [P, S], F32)
        rcos = at("P", "rcos", [P, S], F32)
        silu = at("P", "silu", [P, 2, S], F32)
        nmax = at("P", "nmax", [P, 2], F32)
        den = at("P", "den", [P, 8], F32)
        rden = at("P", "rden", [P, 8], F32)
        m_hi = at("G", "m_hi", [P, KT, S], F32R)
        m_lo = at("G", "m_lo", [P, KT, S], F32R)
        z_hi = at("G", "z_hi", [P, KT, S], F32R)
        z_lo = at("G", "z_lo", [P, KT, S], F32R)
        pad = top["G"]
        y_hi = at("G", "y_hi", [P, KA, S], F32R)
        y_lo = at("G", "y_lo", [P, KA, S], F32R)
        sA = at("G", "sA", [P, 2, S], F32)
        sB = at("G", "sB", [P, 2, S], F32)
        u_hi, u_lo = z_hi, z_lo
        top["N"] = pad
        ssum = at("N", "ssum", [P, S], F32)
        sq = at("N", "sq", [P, 2, S], F32)
        diag = at("N", "diag", [P, TB, P], F32)
        hn = at("N", "hn", [P, 2, S], F32)
        relu = at("N", "relu", [P, 2, S], F32)
        relu2 = at("N", "relu2", [P, 2, S], F32)
        x_nat = at("X", "x_nat", [P, TB, D], F32)
        mask_in = at("X", "mask_in", [P, TB, S + 2 * P], F32)
        stage = at("Y", "stage", [P, 2, D], F32)
        for k_, v_ in top.items():
            assert v_ <= nc.sbuf_usable_end, (k_, v_, nc.sbuf_usable_end)

        pj = [ps(f"pj{i}", S) for i in range(2)]
        sc = ps("sc", 2 * S)
        pt = ps("pt", 2 * S)
        yo = ps("yo", S)
        rb = ps("rb", S)
        vbank = [sc[:, 0:S], sc[:, S:2 * S], pt[:, 0:S], pt[:, S:2 * S]]

        const_in = sem("const_in")
        ident_in = sem("ident_in")
        tables_in = sem("tables_in")
        tables_done = sem("tables_done")
        const_set = sem("const_set")
        mask_landed = sem("mask_landed")
        mask_set = sem("mask_set")
        x_in = [sem(f"x_in{i}") for i in range(2)]
        x_turned = sem("x_turned")
        x_init = sem("x_init")
        gain_set = sem("gain_set")
        landed = [sem(f"landed{i}") for i in range(2)]
        hi_done = sem("hi_done")
        lo_done = sem("lo_done")
        mm_done = sem("mm_done")
        bank_free = [sem(f"bank_free{i}") for i in range(2)]
        sq_done = sem("sq_done")
        sum_done = sem("sum_done")
        mean_done = sem("mean_done")
        std_done = sem("std_done")
        rstd_done = sem("rstd_done")
        diag_done = sem("diag_done")
        spread_done = sem("spread_done")
        rstd_all_done = sem("rstd_all_done")
        hn_done = sem("hn_done")
        h_hi_done = sem("h_hi_done")
        h_ready = sem("h_ready")
        v_done = sem("v_done")
        v_out = sem("v_out")
        rot_swap = sem("rot_swap")
        rot_sin = sem("rot_sin")
        rot_cos = sem("rot_cos")
        rot_out = sem("rot_out")
        att_qk = sem("att_qk")
        att_masked = sem("att_masked")
        att_exp = sem("att_exp")
        att_turned = sem("att_turned")
        att_probT = sem("att_probT")
        att_pv = sem("att_pv")
        att_rden = sem("att_rden")
        att_y = sem("att_y")
        y_turned = sem("y_turned")
        y_out = sem("y_out")
        decay_in = sem("decay_in")
        st_mm = sem("st_mm")
        st_out = sem("st_out")
        ret_mm = sem("ret_mm")
        ret_sq = sem("ret_sq")
        ret_out = sem("ret_out")
        ret_sum = sem("ret_sum")
        ret_mean = sem("ret_mean")
        ret_std = sem("ret_std")
        ret_rstd = sem("ret_rstd")
        ret_scaled = sem("ret_scaled")
        z_done = sem("z_done")
        g_sigmoid = sem("g_sigmoid")
        silu_done = sem("silu_done")
        gate_sigmoid = sem("gate_sigmoid")
        relu_scaled = sem("relu_scaled")
        split_hi = sem("split_hi")
        split_done = sem("split_done")
        merged = sem("merged")
        m_hi_done = sem("m_hi_done")
        m_ready = sem("m_ready")
        relu2_done = sem("relu2_done")
        u_hi_done = sem("u_hi_done")
        u_ready = sem("u_ready")
        f_done = sem("f_done")
        f_turned = sem("f_turned")
        f_staged = sem("f_staged")
        out_done = [sem(f"out_done{i}") for i in range(2)]

        st0 = [sum(S - P * i for i in range(j)) for j in range(TB)]

        def by_residue(v):
            return v.rearrange("p (m r) -> p r m", r=4)

        block = ctx.enter_context(nc.Block())

        w_in_t = a["w_in"].rearrange("l (k p) (t c) -> l p k t c", p=P, c=P)
        w_in_u = a["w_in"].rearrange("l (k p) (t c) -> l p k t c", p=P, c=2 * P)
        w_in_v = a["w_in"].rearrange("l (k p) (t c) -> l p k t c", p=P, c=4 * P)
        w_a_u = a["w_a"].rearrange("l (k p) (t c) -> l p k t c", p=P, c=2 * P)
        w_b_u = a["w_b"].rearrange("l (k p) (t c) -> l p k t c", p=P, c=2 * P)
        w_o_u = a["w_o"].rearrange("l (k p) (t c) -> l p k t c", p=P, c=2 * P)
        w_up_u = a["w_up"].rearrange("l (k p) (t c) -> l p k t c", p=P, c=2 * P)
        w_down_u = a["w_down"].rearrange("l (f k p) (t c) -> l p f k t c", p=P, k=KT, c=2 * P)

        @block.sync
        def _(sp):
            sp.dma_start(ident[:], a["ident"]).then_inc(ident_in, 16)
            for i in range(2):
                c = slice(i * D // 2, (i + 1) * D // 2)
                sp.dma_start(x_nat[:, :, c], a["x"].rearrange("b (t p) d -> p (b t) d", p=P)[:, :, c]).then_inc(x_in[i], 16)
            sp.dma_start(gains[:], a["gains"]).then_inc(const_in, 16)

            def load(n, s, halves):
                sp.wait_ge(lo_done, n - 2 + 1 + UNIT_CREDIT)
                for dst, src in halves:
                    sp.dma_start(dst, src).then_inc(landed[s], 16)

            def tiles(s, v, t0, t1):
                d = raw[s][:].rearrange("p (k o c) -> p k o c", o=2, c=P)
                return [(d[:, :, 0, :], v[:, :, t0, :]), (d[:, :, 1, :], v[:, :, t1, :])]

            def cols(s, v, t, kt=KT):
                d = raw[s][:].rearrange("p (k c) -> p k c", k=KT)
                m = kt // 2
                return [(d[:, 0:m, :], v[:, 0:m, t, :]), (d[:, m:kt, :], v[:, m:kt, t, :])]

            with sp.Fori(0, DEPTH) as l:
                with sp.Fori(0, GROUPS) as g:
                    for u in range(V_U):
                        d = raw[u][:].rearrange("p (k c) -> p k c", k=4)
                        load(l * LU + V0 + g * V_U + u, u,
                             [(d[:, m:m + 2, :], w_in_v[l, :, 4 * u + m:4 * u + m + 2, 2 * GROUPS + g, :])
                              for m in (0, 2)])
                sp.wait_ge(rot_out, l * 8 * PAIRS + 1)
                sp.dma_start(tables[:], a["tables"]).then_inc(tables_in, 16)
                with sp.Fori(0, PAIRS) as i:
                    n = l * LU + P0 + i * P_U
                    for g in range(GROUPS):
                        load(n + g, g % 2, tiles(g % 2, w_in_t[l], PAIRS * g + i, PAIRS * (GROUPS + g) + i))
                    load(n + 3, 1, tiles(1, w_in_t[l], COL_QR // P + i, COL_QR // P + RH + i))
                    load(n + 4, 0, cols(0, w_in_u[l], COL_VR // 256 + i))
                    sp.wait_ge(st_out, (l * PAIRS + i) * TB + 1)
                    sp.dma_start(decay[:], a["decay"][i]).then_inc(decay_in, 16)
                    load(n + 5, 1, cols(1, w_in_u[l], COL_GR // 256 + i))
                with sp.Fori(0, 4) as p:
                    n = l * LU + G0 + p * G_U
                    load(n + 0, 0, cols(0, w_in_u[l], COL_GA // 256 + p))
                    load(n + 1, 1, cols(1, w_in_u[l], COL_GB // 256 + p))
                    load(n + 2, 0, cols(0, w_b_u[l], p))
                    load(n + 3, 1, cols(1, w_a_u[l], p, KA))
                with sp.Fori(0, 2) as i:
                    for u in range(O_U):
                        load(l * LU + O0 + i * O_U + u, u, cols(u, w_o_u[l], 2 * i + u))
                with sp.Fori(0, CH) as c:
                    n = l * LU + M0 + c * M_U
                    for u in range(4):
                        load(n + u, u % 2, cols(u % 2, w_up_u[l], 4 * c + u))
                    for u in range(4):
                        load(n + 4 + u, u % 2, cols(u % 2, w_down_u[l, :, c], u))
            sp.wait_ge(lo_done, DEPTH * LU - 1 + UNIT_CREDIT)
            sp.sem_inc(landed[0], 32)

            out_v = a["out"].rearrange("b (t p) d -> (b t) p d", p=P)
            for b in range(TB):
                sp.wait_ge(f_staged, b + 1)
                sp.dma_start(out_v[b], stage[:, b % 2, :]).then_inc(out_done[b % 2], 16)
            for s in out_done:
                sp.wait_ge(s, 16 * TB // 2)

        @block.scalar
        def _(act):
            act.wait_ge(const_set, 4)

            def split_unit(half, n, s):
                act.wait_ge(landed[s], half * 32 + 32)
                act.wait_ge(mm_done, n * 2 - 2 + MM_CREDIT)
                nc.scalar.copy(w_hi[s][:], raw[s][:]).then_inc(hi_done, 1)

            def ahead(l, base, per, i, u):
                k = u + 1
                split_unit(l * (LU // 2) + base // 2 + i * (per // 2) + k // 2, l * LU + base + i * per + k, k % 2)

            def banks(l, base, per, i, u):
                return l * LQ + base - P0 + i * per + u

            def square_and_split(J, k):
                if k >= 2:
                    act.wait_ge(sum_done, J * (KT - 1) + max(k - 2, 1))
                nc.scalar.activation(sq[:, k % 2, :], x[:, k, :], ACT.Square).then_inc(sq_done, 1)
                act.wait_ge(hn_done, J * KT + k + 1)
                nc.scalar.copy(h_hi[:, k, :], hn[:, k % 2, :]).then_inc(h_hi_done, 1)

            def rms(J):
                act.wait_ge(mean_done, J + 1)
                nc.scalar.activation(std[:], rb[:, 0:2 * TB], ACT.Sqrt, bias=eps[:]).then_inc(std_done, 1)

            for k in range(KT):
                act.wait_ge(x_turned, k + 1)
                nc.scalar.copy(x[:, k, :], pj[k % 2][:]).then_inc(x_init, 1)
                if k == 1:
                    act.wait_ge(landed[0], 32)
                    nc.scalar.copy(w_hi[0][:], raw[0][:]).then_inc(hi_done, 1)
                act.wait_ge(x_init, k + 1)
                square_and_split(0, k)

            with act.Fori(0, DEPTH) as l:
                ahead(l, V0, V_U, 0, 0)
                rms(2 * l)
                with act.Fori(0, GROUPS - 1) as g:
                    ahead(l, V0, V_U, g, 1)
                    ahead(l, V0, V_U, g, 2)
                ahead(l, V0, V_U, GROUPS - 1, 1)
                with act.Fori(0, PAIRS) as i:
                    J = l * PAIRS + i
                    n = l * LU + P0 + i * P_U
                    q = banks(l, P0, P_U, i, 0)

                    def tile(u, o):
                        act.wait_ge(mm_done, (n + u) * 2 + o + 1 + MM_CREDIT)

                    def rot_in(u, o):
                        t = 2 * u + o
                        tile(u, o)
                        act.wait_ge(rot_out, J * 8 + t + 1)
                        if u < GROUPS:
                            nc.scalar.copy(rot[0][:], pj[o][:]).then_inc(bank_free[o], 1)
                        else:
                            nc.scalar.copy(rot[0][:], pj[o][:])
                            nc.scalar.copy(swp[0:64, :], pj[o][64:128, :])
                            nc.scalar.copy(swp[64:128, :], pj[o][0:64, :]).then_inc(bank_free[o], 1)

                    def exp(b):
                        act.wait_ge(att_masked, J * 8 + b + 1)
                        nc.scalar.activation(prob[0][:], prob[0][:], ACT.Exp, scale=-1.0,
                                             bias=nmax[:, b % 2:b % 2 + 1],
                                             accum_out=den[:, b:b + 1]).then_inc(att_exp, 1)

                    def probT_out(b):
                        act.wait_ge(att_turned, J * 8 + b + 1)
                        if b >= 1:
                            act.wait_ge(att_pv, J * 8 + b)
                        nc.scalar.copy(probT[:], pt[:, 0:S + 2 * P]).then_inc(att_probT, 1)

                    for u in range(GROUPS):
                        ahead(l, P0, P_U, i, u)
                        rot_in(u, 0)
                        rot_in(u, 1)
                    ahead(l, P0, P_U, i, 3)
                    exp(0)
                    rot_in(3, 0)
                    probT_out(0)
                    exp(1)
                    probT_out(1)
                    exp(2)
                    ahead(l, P0, P_U, i, 4)
                    rot_in(3, 1)
                    probT_out(2)
                    exp(3)
                    probT_out(3)
                    exp(4)

                    def vR_out(o):
                        tile(4, o)
                        if o == 0:
                            act.wait_ge(ret_mm, J * 2 + 1 + 1)
                        for half in range(2):
                            b = 2 * o + half
                            mm = nc.scalar.activation(vR[:, b, :], pj[o][:, half * RV:(half + 1) * RV], ACT.Copy,
                                                      scale=rstd[:, b:b + 1])
                        mm.then_inc(bank_free[o], 1)

                    vR_out(0)
                    probT_out(4)
                    exp(5)
                    probT_out(5)
                    exp(6)
                    ahead(l, P0, P_U, i, 5)
                    vR_out(1)
                    probT_out(6)
                    exp(7)
                    probT_out(7)

                    def ret_square(e):
                        act.wait_ge(ret_out, J * 2 + e + 1)
                        nc.scalar.activation(sqR[e], rb[:],
                                             ACT.Square).then_inc(ret_sq, 1)

                    def gate_sig(o):
                        act.wait_ge(bank_free[o], q + 6 + BANK_CREDIT)
                        nc.scalar.activation(sigR[o], silu[:, o, :], ACT.Sigmoid).then_inc(g_sigmoid, 1)

                    sigR = [swp[:], prob[0][:, 0:S]]
                    sqR = [probT[:, 0:S], rot[0][:]]
                    act.wait_ge(att_pv, J * 8 + 8)
                    ret_square(0)
                    gate_sig(0)
                    ret_square(1)
                    gate_sig(1)
                    act.wait_ge(ret_mean, J + 1)
                    nc.scalar.activation(probT[:, 0:S], rb[:], ACT.Sqrt, bias=eps[:]).then_inc(ret_std, 1)
                def split_z(ks):
                    for k in ks:
                        nc.scalar.copy(z_hi[:, k, :], z[:, k, :]).then_inc(split_hi, 1)

                def gate(p, u, o):
                    act.wait_ge(bank_free[o], l * LQ + G0 - P0 + p * G_U + u + 1 + BANK_CREDIT)
                    dst = (sA, sB)[u]
                    nc.scalar.activation(dst[:, o, :], dst[:, o, :], ACT.Sigmoid).then_inc(gate_sigmoid, 1)

                ahead(l, G0, G_U, 0, 0)
                act.wait_ge(y_out, l * PAIRS + PAIRS + 1)
                for k in range(KA):
                    nc.scalar.copy(y_hi[:, k, :], yA[:, k, :]).then_inc(split_hi, 1)
                act.wait_ge(z_done, l * KT + KT)
                for u in range(2):
                    for o in range(2):
                        gate(0, u, o)
                        split_z(range(4 * u + 2 * o, 4 * u + 2 * o + 2))
                    if u == 0:
                        ahead(l, G0, G_U, 0, 1)
                with act.Fori(0, 3) as p:
                    ahead(l, G0, G_U, p, 2)
                    ahead(l, G0, G_U, p, 3)
                    for u in range(2):
                        ahead(l, G0, G_U, p, 4 + u)
                        for o in range(2):
                            gate(p + 1, u, o)
                ahead(l, G0, G_U, 3, 2)
                ahead(l, G0, G_U, 3, 3)
                def added(u, o, count):
                    act.wait_ge(bank_free[o], count + BANK_CREDIT)

                for u in range(4):
                    ahead(l, O0, O_U, 0, u)
                    for o in range(2):
                        added(u, o, l * LQ + O0 - P0 + u + 1)
                        square_and_split(2 * l + 1, 2 * u + o)
                def relu_out(c, u, o):
                    act.wait_ge(mm_done, (l * LU + M0 + c * M_U + u) * 2 + o + 1 + MM_CREDIT)
                    nc.scalar.activation(relu[:, o, :], pj[o][:], ACT.Relu).then_inc(bank_free[o], 1)

                def u_split(c, u, o):
                    t = 2 * u + o if u < 8 else 8 + o
                    act.wait_ge(relu2_done, (l * CH + c) * 8 + t + 1)
                    nc.scalar.copy(u_hi[:, t % 8, :], relu2[:, o, :]).then_inc(u_hi_done, 1)

                def up(c, u):
                    ahead(l, M0, M_U, c, u)
                    for o in range(2):
                        relu_out(c, u, o)
                        u_split(c, u, o)

                ahead(l, M0, M_U, 0, 0)
                relu_out(0, 0, 0)
                rms(2 * l + 1)
                relu_out(0, 0, 1)
                u_split(0, 0, 0)
                u_split(0, 0, 1)
                with act.Fori(0, CH - 1) as c:
                    for u in (1, 2, 3):
                        up(c, u)
                    for u in (4, 5, 6, 7):
                        ahead(l, M0, M_U, c, u)
                    up(c, 8)
                for u in (1, 2, 3):
                    up(CH - 1, u)
                for u in (4, 5, 6, 7):
                    ahead(l, M0, M_U, CH - 1, u)
                    for o in range(2):
                        added(u, o, l * LQ + M0 - P0 + (CH - 1) * M_U + u + 1)
                        square_and_split(2 * l + 2, 2 * (u - 4) + o)
            rms(2 * DEPTH)
            for b in range(TB):
                act.wait_ge(rstd_done, 2 * DEPTH + 1)
                act.wait_ge(f_turned, b + 1)
                if b >= 2:
                    act.wait_ge(out_done[b % 2], 16 * (b // 2))
                nc.scalar.activation(stage[:, b % 2, :], (sc, pt)[b % 2][:], ACT.Copy,
                                     scale=rstd[:, b:b + 1]).then_inc(f_staged, 1)

        @block.gpsimd
        def _(pool):
            nc.gpsimd.memset(ones[:], 1.0).then_inc(const_set, 1)
            nc.gpsimd.memset(inv_d[:], 1.0 / D).then_inc(const_set, 1)
            nc.gpsimd.memset(ones_r[:], 1.0 / RV).then_inc(const_set, 1)
            nc.gpsimd.memset(eps[:], EPS).then_inc(const_set, 1)
            pool.sem_inc(lo_done, UNIT_CREDIT)

            def lo(n, s):
                pool.wait_ge(hi_done, n + 1)
                nc.gpsimd.tensor_tensor(w_lo[s][:], raw[s][:], w_hi[s][:], ALU.subtract).then_inc(lo_done, 1)

            lo(0, 0)
            pool.dma_start(mask_in[:], a["mask"]).then_inc(mask_landed, 16)
            with pool.Fori(0, DEPTH) as l:
                with pool.Fori(0, GROUPS) as g:
                    for u in range(V_U):
                        lo(l * LU + V0 + g * V_U + u + 1, (u + 1) % 2)
                with pool.Fori(0, PAIRS) as i:
                    J = l * PAIRS + i
                    n = l * LU + P0 + i * P_U
                    q = l * LQ + i * P_U
                    for u in range(P_U):
                        lo(n + u + 1, (u + 1) % 2)
                        for o in range(2 if u < 4 else 0):
                            pool.wait_ge(bank_free[o], q + u + 1 + BANK_CREDIT)
                            pool.wait_ge(rot_out, J * 8 + 2 * u + o + 1)
                            pool.wait_ge(tables_done, l + 1)
                            nc.gpsimd.tensor_tensor(rcos[:], rot[0][:], cosA if u < 3 else cosR,
                                                    ALU.mult).then_inc(rot_cos, 1)
                with pool.Fori(0, (LU - G0) // 2) as j:
                    for u in range(2):
                        lo(l * LU + G0 + 2 * j + u + 1, (u + 1) % 2)

        @block.vector
        def _(dve):
            for s in bank_free:
                dve.sem_inc(s, BANK_CREDIT)
            dve.sem_inc(rot_out, 1)
            dve.sem_inc(y_out, 1)
            dve.sem_inc(ret_std, 1)
            dve.sem_inc(st_out, 1)
            dve.sem_inc(v_out, TB)
            dve.sem_inc(m_ready, 2)

            def scale_and_split(J, k, g):
                if k >= 2:
                    dve.wait_ge(h_ready, J * KT + k - 1)
                nc.vector.tensor_scalar(hn[:, k % 2, :], x[:, k, :], g[:, k:k + 1], None,
                                        ALU.mult).then_inc(hn_done, 1)
                if k >= 1:
                    dve.wait_ge(sq_done, J * KT + k + 1)
                    if k > 1:
                        dve.wait_ge(sum_done, J * (KT - 1) + k - 1)
                    nc.vector.tensor_tensor(ssum[:], sq[:, 0, :] if k == 1 else ssum[:], sq[:, k % 2, :],
                                            ALU.add).then_inc(sum_done, 1)
                dve.wait_ge(h_hi_done, J * KT + k + 1)
                nc.vector.tensor_tensor(h_lo[:, k, :], hn[:, k % 2, :], h_hi[:, k, :],
                                        ALU.subtract).then_inc(h_ready, 1)

            def rms(J, squared=False):
                dve.wait_ge(std_done, J + 1)
                nc.vector.reciprocal(rstd[:], std[:]).then_inc(rstd_done, 1)
                dve.wait_ge(rstd_done, J + 1)
                for b in range(TB):
                    r = rstd[:, b:b + 1]
                    mm = nc.vector.tensor_scalar(diag[:, b, :], ident[:], r, r if squared else None, ALU.mult,
                                                 ALU.mult if squared else ALU.bypass)
                mm.then_inc(diag_done, 1)

            def rms_spread(J):
                dve.wait_ge(spread_done, J + 1)
                nc.vector.tensor_copy(rstd_all[:], rb[:]).then_inc(rstd_all_done, 1)
                dve.wait_ge(rstd_all_done, J + 1)

            dve.wait_ge(ident_in, 16)
            for k in range(KT):
                dve.wait_ge(x_init, k + 1)
                if k == 0:
                    dve.wait_ge(const_in, 16)
                scale_and_split(0, k, gains[:, 0, :])
            dve.wait_ge(mask_landed, 16)
            nc.vector.tensor_copy(mask[:], mask_in[:]).then_inc(mask_set, 1)

            with dve.Fori(0, DEPTH) as l:
                nc.vector.tensor_scalar(gain[:].rearrange("p w k -> p (w k)"),
                                        gains[:, bass.ds(l * 2 + 1, 2), :].rearrange("p w k -> p (w k)"), 1.0, None,
                                        ALU.mult).then_inc(gain_set, 1)
                rms(2 * l)
                with dve.Fori(0, GROUPS) as g:
                    J = l * GROUPS + g
                    for b in range(TB):
                        if b < TB - 1:
                            dve.wait_ge(v_done, J * (TB - 1) + b + 1)
                        else:
                            dve.wait_ge(mm_done, (l * LU + V0 + g * V_U + 2) * 2 + MM_CREDIT)
                        nc.vector.tensor_scalar(vA[:, b, bass.ds(g * 512, 512)], vbank[b],
                                                rstd[:, TB + b:TB + b + 1], None, ALU.mult).then_inc(v_out, 1)
                rms_spread(2 * l)
                dve.wait_ge(tables_in, l * 16 + 16)
                for i in range(4):
                    mm = nc.vector.tensor_tensor(tables[:, i, :], tables[:, i, :], rstd_all[:], ALU.mult)
                mm.then_inc(tables_done, 1)
                with dve.Fori(0, PAIRS) as i:
                    J = l * PAIRS + i
                    n = l * LU + P0 + i * P_U
                    q = l * LQ + i * P_U

                    def rotary(u, o):
                        t = 2 * u + o
                        dve.wait_ge(bank_free[o], q + u + 1 + BANK_CREDIT)
                        if t == 0:
                            dve.wait_ge(tables_done, l + 1)
                        if u < GROUPS:
                            nc.vector.memset(tick[:], 0.0)
                            nc.vector.stream_shuffle(swp[:], rot[0][:], SHUFFLE).then_inc(rot_swap, 1)
                            dve.wait_ge(rot_swap, J * 6 + t + 1)
                        nc.vector.tensor_tensor(swp[:], swp[:], sinA if u < GROUPS else sinR,
                                                ALU.mult).then_inc(rot_sin, 1)
                        dve.wait_ge(rot_sin, J * 8 + t + 1)
                        dve.wait_ge(rot_cos, J * 8 + t + 1)
                        if u < GROUPS:
                            nc.vector.tensor_tensor(qk[:, t, :].rearrange("p (r m) -> p r m", r=4),
                                                    by_residue(rcos[:]), by_residue(swp[:]),
                                                    ALU.add).then_inc(rot_out, 1)
                        else:
                            nc.vector.tensor_tensor(qkR[:, o, :], rcos[:], swp[:], ALU.add).then_inc(rot_out, 1)

                    def masked(b):
                        if b == 0:
                            dve.wait_ge(mask_set, 1)
                        dve.wait_ge(att_qk, J * 8 + b + 1)
                        if b >= 1:
                            dve.wait_ge(att_turned, J * 8 + b)
                        nc.vector.memset(tick[:], 0.0)
                        nc.vector.tensor_tensor_reduce(
                            out=prob[0][:], in0=sc[:, 0:S + 2 * P], in1=mask[:, b // 2, :],
                            scale=-(DH ** -0.5), scalar=3e38, op0=ALU.add, op1=ALU.min,
                            accum_out=nmax[:, b % 2:b % 2 + 1]).then_inc(att_masked, 1)

                    def y_block(b):
                        dve.wait_ge(att_exp, J * 8 + b + 1)
                        nc.vector.reciprocal(rden[:, b:b + 1], den[:, b:b + 1]).then_inc(att_rden, 1)
                        dve.wait_ge(att_pv, J * 8 + b + 1)
                        dve.wait_ge(att_rden, J * 8 + b + 1)
                        c = (b % 2) * DH
                        nc.vector.tensor_scalar(ysb[:, b // 2, c:c + DH],
                                                yo[:, (b // 2) * P + c:(b // 2) * P + c + DH],
                                                rden[:, b:b + 1], None, ALU.mult).then_inc(att_y, 1)

                    def st_decayed(j):
                        dve.wait_ge(st_mm, J * TB + j + 1)
                        w = S - j * P
                        if j == 0:
                            dve.wait_ge(decay_in, J * 16 + 16)
                        nc.vector.tensor_tensor(ST[:, st0[j]:st0[j] + w], rb[:, 0:w], decay[:, 0:w],
                                                ALU.mult).then_inc(st_out, 1)

                    def ret_copy(e):
                        dve.wait_ge(ret_mm, J * 2 + e + 1 + 2)
                        nc.vector.tensor_scalar(z[:, bass.ds(2 * i + e, 1), :].rearrange("p k s -> p (k s)"),
                                                rb[:], 1.0, None, ALU.mult).then_inc(ret_out, 1)

                    def gate_scale(o):
                        dve.wait_ge(mm_done, (n + 5) * 2 + o + 1 + MM_CREDIT)
                        nc.vector.tensor_tensor(silu[:, o, :], pj[o][:], rstd_all[:], ALU.mult).then_inc(bank_free[o], 1)

                    def silu_gate(o):
                        dve.wait_ge(g_sigmoid, J * 2 + o + 1)
                        nc.vector.tensor_tensor(silu[:, o, :], silu[:, o, :], (swp[:], prob[0][:, 0:S])[o],
                                                ALU.mult).then_inc(silu_done, 1)

                    for t in range(6):
                        rotary(t // 2, t % 2)
                    masked(0)
                    rotary(3, 0)
                    masked(1)
                    y_block(0)
                    masked(2)
                    y_block(1)
                    masked(3)
                    rotary(3, 1)
                    for s in range(4):
                        y_block(2 + s)
                        masked(4 + s)
                        st_decayed(s)
                    y_block(6)
                    ret_copy(0)
                    y_block(7)
                    gate_scale(0)
                    ret_copy(1)
                    silu_gate(0)
                    dve.wait_ge(ret_sq, J * 2 + 2)
                    nc.vector.tensor_tensor(rcos[:], probT[:, 0:S], rot[0][:], ALU.add).then_inc(ret_sum, 1)
                    gate_scale(1)
                    dve.wait_ge(y_turned, J + 1)
                    nc.vector.tensor_scalar(
                        yA[:, bass.ds(i, 1), :].rearrange("p k (m r) -> p (k m) r", r=4),
                        yo[:].rearrange("p (r m) -> p m r", r=4), 1.0, None, ALU.mult).then_inc(y_out, 1)
                    silu_gate(1)
                    dve.wait_ge(ret_std, J + 1 + 1)
                    nc.vector.reciprocal(probT[:, 0:S], probT[:, 0:S]).then_inc(ret_rstd, 1)
                    dve.wait_ge(ret_rstd, J + 1)
                    for e in range(2):
                        ze = z[:, bass.ds(2 * i + e, 1), :].rearrange("p k s -> p (k s)")
                        dve.wait_ge(silu_done, J * 2 + e + 1)
                        nc.vector.tensor_tensor(silu[:, e, :], silu[:, e, :], probT[:, 0:S],
                                                ALU.mult).then_inc(ret_scaled, 1)
                        dve.wait_ge(ret_scaled, J * 2 + e + 1)
                        nc.vector.tensor_tensor(ze, ze, silu[:, e, :], ALU.mult).then_inc(z_done, 1)
                def split(k, lo_, src, hi_, count):
                    dve.wait_ge(split_hi, l * (KT + KA) + count + 1)
                    nc.vector.tensor_tensor(lo_[:, k, :], src[:, k, :], hi_[:, k, :],
                                            ALU.subtract).then_inc(split_done, 1)

                def gate(p, u, o):
                    dve.wait_ge(mm_done, (l * LU + G0 + p * G_U + u) * 2 + o + 1 + MM_CREDIT)
                    dve.wait_ge(m_ready, (l * 4 + p) * 2 + o + 1)
                    nc.vector.tensor_tensor((sA, sB)[u][:, o, :], pj[o][:], rstd_all[:],
                                            ALU.mult).then_inc(bank_free[o], 1)

                def merge(p):
                    J = l * 4 + p
                    n = l * LU + G0 + p * G_U
                    q = l * LQ + G0 - P0 + p * G_U
                    for u, dst in ((2, sB), (3, sA)):
                        for o in range(2):
                            dve.wait_ge(gate_sigmoid, J * 4 + 4)
                            dve.wait_ge(mm_done, (n + u) * 2 + o + 1 + MM_CREDIT)
                            nc.vector.tensor_tensor(dst[:, o, :], pj[o][:], dst[:, o, :],
                                                    ALU.mult).then_inc(bank_free[o], 1)
                    for o in range(2):
                        dve.wait_ge(bank_free[o], q + 4 + BANK_CREDIT)
                        nc.vector.tensor_tensor(sA[:, o, :], sA[:, o, :], sB[:, o, :], ALU.add).then_inc(merged, 1)
                    for o in range(2):
                        at_ = 2 * p + o
                        if isinstance(p, int):
                            mh, ml = m_hi[:, at_, :], m_lo[:, at_, :]
                        else:
                            mh, ml = (m[:, bass.ds(at_, 1), :].rearrange("p k s -> p (k s)") for m in (m_hi, m_lo))
                        dve.wait_ge(merged, J * 2 + o + 1)
                        nc.vector.tensor_scalar(mh, sA[:, o, :], 1.0, None, ALU.mult).then_inc(m_hi_done, 1)
                        dve.wait_ge(m_hi_done, J * 2 + o + 1)
                        nc.vector.tensor_tensor(ml, sA[:, o, :], mh, ALU.subtract).then_inc(m_ready, 1)

                for k in range(KA):
                    split(k, y_lo, yA, y_hi, k)
                for u in range(2):
                    for o in range(2):
                        gate(0, u, o)
                        for k in range(4 * u + 2 * o, 4 * u + 2 * o + 2):
                            split(k, z_lo, z, z_hi, KA + k)
                with dve.Fori(0, 3) as p:
                    merge(p)
                    for u in range(2):
                        for o in range(2):
                            gate(p + 1, u, o)
                merge(3)
                def x_add(n, t, o):
                    dve.wait_ge(mm_done, n * 2 + o + 1 + MM_CREDIT)
                    nc.vector.tensor_tensor(x[:, t, :], pj[o][:], x[:, t, :], ALU.add).then_inc(bank_free[o], 1)

                dve.wait_ge(gain_set, l + 1)
                for u in range(4):
                    for o in range(2):
                        x_add(l * LU + O0 + u, 2 * u + o, o)
                        dve.wait_ge(bank_free[o], l * LQ + O0 - P0 + u + 1 + BANK_CREDIT)
                        scale_and_split(2 * l + 1, 2 * u + o, gain[:, 0, :])
                def relu_square(c, u, o):
                    t = 2 * u + o if u < 8 else 8 + o
                    dve.wait_ge(bank_free[o], l * LQ + M0 - P0 + c * M_U + u + 1 + BANK_CREDIT)
                    nc.vector.tensor_tensor(relu2[:, o, :], relu[:, o, :], rstd_all[:], ALU.mult).then_inc(relu_scaled, 1)
                    dve.wait_ge(relu_scaled, (l * CH + c) * 8 + t + 1)
                    nc.vector.tensor_tensor(relu2[:, o, :], relu2[:, o, :], relu[:, o, :],
                                            ALU.mult).then_inc(relu2_done, 1)
                    dve.wait_ge(u_hi_done, (l * CH + c) * 8 + t + 1)
                    nc.vector.tensor_tensor(u_lo[:, t % 8, :], relu2[:, o, :], u_hi[:, t % 8, :],
                                            ALU.subtract).then_inc(u_ready, 1)

                rms(2 * l + 1, squared=True)
                rms_spread(2 * l + 1)
                for o in range(2):
                    relu_square(0, 0, o)
                with dve.Fori(0, CH - 1) as c:
                    for u in (1, 2, 3, 4, 5, 6, 7, 8):
                        for o in range(2):
                            if 4 <= u < 8:
                                x_add(l * LU + M0 + c * M_U + u, 2 * (u - 4) + o, o)
                            else:
                                relu_square(c, u, o)
                for u in (1, 2, 3):
                    for o in range(2):
                        relu_square(CH - 1, u, o)
                for u in (4, 5, 6, 7):
                    for o in range(2):
                        t = 2 * (u - 4) + o
                        x_add(l * LU + M0 + (CH - 1) * M_U + u, t, o)
                        dve.wait_ge(bank_free[o], l * LQ + M0 - P0 + (CH - 1) * M_U + u + 1 + BANK_CREDIT)
                        scale_and_split(2 * l + 2, t, gain[:, 1, :])
            for k in range(KT):
                nc.vector.tensor_scalar(x[:, k, :], x[:, k, :], gains[:, 2 * DEPTH, k:k + 1], None,
                                        ALU.mult).then_inc(f_done, 1)
            dve.wait_ge(std_done, 2 * DEPTH + 1)
            nc.vector.reciprocal(rstd[:], std[:]).then_inc(rstd_done, 1)

        @block.tensor
        def _(pe):
            pe.sem_inc(mm_done, MM_CREDIT)
            pe.sem_inc(ret_mm, 2)
            pe.wait_ge(ident_in, 16)
            pe.wait_ge(const_set, 4)
            for k in range(KT):
                if k % (KT // 2) == 0:
                    pe.wait_ge(x_in[k // (KT // 2)], 16)
                if k >= 2:
                    pe.wait_ge(x_init, k - 1)
                for b in range(TB):
                    last = nc.tensor.transpose(pj[k % 2][:, b * P:(b + 1) * P], x_nat[:, b, k * P:(k + 1) * P],
                                               ident[:])
                last.then_inc(x_turned, 1)

            def mean(J):
                pe.wait_ge(sum_done, (J + 1) * (KT - 1))
                for b in range(TB):
                    nc.tensor.matmul(rb[:, b:b + 1], ssum[:, b * P:(b + 1) * P], inv_d[:], start=True, stop=True)
                for b in range(TB):
                    mm = nc.tensor.matmul(rb[:, TB + b:TB + b + 1], by_residue(ssum[:])[:, b], inv_d[:],
                                          start=True, stop=True)
                mm.then_inc(mean_done, 1)

            def spread(J):
                pe.wait_ge(diag_done, J + 1)
                for b in range(TB):
                    mm = nc.tensor.matmul(rb[:, b * P:(b + 1) * P], ones[:], diag[:, b, :], start=True, stop=True)
                mm.then_inc(spread_done, 1)

            def weights(n):
                pe.wait_ge(lo_done, n + 1 + UNIT_CREDIT)

            def three(out, s, wc, acts, first, last):
                nc.tensor.matmul(out, w_hi[s][:, wc], acts[0], start=first, stop=False)
                nc.tensor.matmul(out, w_hi[s][:, wc], acts[1], start=False, stop=False)
                return nc.tensor.matmul(out, w_lo[s][:, wc], acts[0], start=False, stop=last)

            def tile_half(s, o, acts, ks, kt=KT, ready=None):
                for k in ks:
                    if ready:
                        ready(k)
                    mm = three(pj[o][:], s, slice(k * 256 + o * P, k * 256 + o * P + P),
                               (acts[0][:, k, :], acts[1][:, k, :]), k == 0, k == kt - 1)
                if ks[-1] == kt - 1:
                    mm.then_inc(mm_done, 1)

            def unit(n, q, s, acts, kt=KT, ready=None, behind=(None, None)):
                weights(n)
                for o in range(2):
                    pe.wait_ge(bank_free[o], q + BANK_CREDIT)
                    tile_half(s, o, acts, range(kt), kt, ready if o == 0 else None)
                    if behind[o]:
                        behind[o]()

            h = (h_hi, h_lo)
            with pe.Fori(0, DEPTH) as l:
                def values_half(g, u):
                    weights(l * LU + V0 + g * V_U + u)
                    for kk in range(4):
                        k = 4 * u + kk
                        if isinstance(g, int) and g == 0:
                            pe.wait_ge(h_ready, l * 2 * KT + k + 1)
                        w = slice(kk * 512, kk * 512 + 512)
                        for b in range(TB):
                            if k == 0:
                                pe.wait_ge(v_out, (l * GROUPS + g) * TB + b + 1)
                            hh, hl = by_residue(h_hi[:, k, :])[:, b], by_residue(h_lo[:, k, :])[:, b]
                            nc.tensor.matmul(vbank[b], hh, w_hi[u][:, w], start=(k == 0), stop=False)
                            nc.tensor.matmul(vbank[b], hh, w_lo[u][:, w], start=False, stop=False)
                            mm = nc.tensor.matmul(vbank[b], hl, w_hi[u][:, w], start=False, stop=(k == KT - 1))
                            if k == KT - 1 and b < TB - 1:
                                mm.then_inc(v_done, 1)
                    mm.then_inc(mm_done, 2)

                values_half(0, 0)
                for k in range(4, KT):
                    pe.wait_ge(h_ready, l * 2 * KT + k + 1)
                mean(2 * l)
                with pe.Fori(0, GROUPS - 1) as g:
                    values_half(g, 1)
                    values_half(g + 1, 0)
                values_half(GROUPS - 1, 1)
                spread(2 * l)
                with pe.Fori(0, PAIRS) as i:
                    J = l * PAIRS + i
                    n = l * LU + P0 + i * P_U
                    q = l * LQ + i * P_U

                    off = [[pe.snap(i * P + (g * AW + hh * DH)) for hh in range(2)] for g in range(GROUPS)]

                    def scores(b):
                        r, rows = b // 2, slice((b % 2) * DH, (b % 2) * DH + DH)
                        if b == 0:
                            pe.wait_ge(rot_out, J * 8 + 6 + 1)
                            pe.wait_ge(v_out, l * GROUPS * TB + (GROUPS + 1) * TB)
                        else:
                            pe.wait_ge(att_masked, J * 8 + b)
                        Q = slice(r * P, r * P + P)
                        nc.tensor.matmul(sc[:, 0:S], qk[rows, 0, Q], qk[rows, 1, :], start=True, stop=True)
                        nc.tensor.matmul(sc[:, S:S + P], qk[rows, 2, Q], qk[rows, 3, Q], start=True, stop=True)
                        nc.tensor.matmul(sc[:, S + P:S + 2 * P], qk[rows, 4, Q], qk[rows, 5, Q],
                                         start=True, stop=True).then_inc(att_qk, 1)

                    def turn(b):
                        pe.wait_ge(att_exp, J * 8 + b + 1)
                        if b >= 1:
                            pe.wait_ge(att_probT, J * 8 + b)
                        for j in range(TB + 2):
                            mm = nc.tensor.transpose(pt[:, j * P:(j + 1) * P], prob[0][:, j * P:(j + 1) * P], ident[:])
                        mm.then_inc(att_turned, 1)

                    def values(b):
                        r, hh = b // 2, b % 2
                        out = yo[:, r * P + hh * DH:r * P + hh * DH + DH]
                        if b == 0:
                            pe.wait_ge(y_out, J + 1)
                        else:
                            pe.wait_ge(att_y, J * 8 + b)
                        pe.wait_ge(att_probT, J * 8 + b + 1)
                        for j in range(TB + 2):
                            blk, g = (j, 0) if j < TB else (r, j - TB + 1)
                            mm = nc.tensor.matmul(out, probT[:, j * P:(j + 1) * P],
                                                  vA[:, blk, bass.ds(off[g][hh], DH)],
                                                  start=(j == 0), stop=(j == TB + 1))
                        mm.then_inc(att_pv, 1)

                    def st(j):
                        if j == 0:
                            pe.wait_ge(rot_out, J * 8 + 8 + 1)
                            pe.wait_ge(ret_std, J + 1)
                            pe.wait_ge(rstd_all_done, 2 * l + 1)
                        else:
                            pe.wait_ge(st_out, J * TB + j + 1)
                        nc.tensor.matmul(rb[:, 0:S - j * P], qkR[:, 1, j * P:(j + 1) * P], qkR[:, 0, j * P:S],
                                         start=True, stop=True).then_inc(st_mm, 1)

                    def ret(e):
                        if e == 0:
                            pe.wait_ge(st_out, J * TB + TB + 1)
                            for o in range(2):
                                pe.wait_ge(bank_free[o], q + 5 + BANK_CREDIT)
                        else:
                            pe.wait_ge(ret_out, J * 2 + 1)
                            pe.wait_ge(ret_sq, J * 2 + 1)
                        for j in range(TB):
                            w = S - j * P
                            mm = nc.tensor.matmul(rb[:, j * P:S], vR[:, j, e * P:(e + 1) * P],
                                                  ST[:, st0[j]:st0[j] + w], start=(j == 0), stop=(j == TB - 1))
                        mm.then_inc(ret_mm, 1)

                    for u in range(GROUPS):
                        unit(n + u, q + u, u % 2, h)
                    for s in range(12):
                        u, o, half = 3 + s // 4, s // 2 % 2, s % 2
                        sl = u % 2
                        if s % 4 == 0:
                            weights(n + u)
                        if half == 0:
                            pe.wait_ge(bank_free[o], q + u + BANK_CREDIT)
                        if u != 4:
                            tile_half(sl, o, h, range(4 * half, 4 * half + 4))
                        else:
                            b = 2 * o + half
                            out = pj[o][:, half * RV:(half + 1) * RV]
                            for k in range(KT):
                                w = slice(k * 256, k * 256 + 256)
                                hh, hl = h_hi[:, k, b * P:(b + 1) * P], h_lo[:, k, b * P:(b + 1) * P]
                                nc.tensor.matmul(out, hh, w_hi[sl][:, w], start=(k == 0), stop=False)
                                nc.tensor.matmul(out, hh, w_lo[sl][:, w], start=False, stop=False)
                                mm = nc.tensor.matmul(out, hl, w_hi[sl][:, w], start=False, stop=(k == KT - 1))
                            if half == 1:
                                mm.then_inc(mm_done, 1)
                        if 3 <= s < 11:
                            values(s - 3)
                        if 2 <= s < 10:
                            turn(s - 2)
                        if 1 <= s < 9:
                            scores(s - 1)
                        if 5 <= s < 9:
                            st(s - 5)
                        if 9 <= s < 11:
                            ret(s - 9)
                    pe.wait_ge(att_y, J * 8 + 8)
                    for r in range(TB):
                        mm = nc.tensor.transpose(yo[:, r * P:(r + 1) * P], ysb[:, r, :], ident[:])
                    mm.then_inc(y_turned, 1)
                    pe.wait_ge(ret_sum, J + 1)
                    pe.wait_ge(ret_out, J * 2 + 2)
                    nc.tensor.matmul(rb[:], ones_r[:], rcos[:], start=True, stop=True).then_inc(ret_mean, 1)
                with pe.Fori(0, 4) as p:
                    n = l * LU + G0 + p * G_U
                    q = l * LQ + G0 - P0 + p * G_U
                    unit(n, q, 0, h)
                    unit(n + 1, q + 1, 1, h)
                    unit(n + 2, q + 2, 0, (z_hi, z_lo), KT, lambda k: pe.wait_ge(split_done, l * (KT + KA) + KA + k + 1))
                    unit(n + 3, q + 3, 1, (y_hi, y_lo), KA)
                for u in range(4):
                    unit(l * LU + O0 + u, l * LQ + O0 - P0 + u, u % 2, (m_hi, m_lo), KT,
                         (lambda k: pe.wait_ge(m_ready, l * KT + k + 1 + 2)) if u == 0 else None)

                def mlp(c, us, ready=None, behind=(None, None)):
                    n = l * LU + M0 + c * M_U
                    q = l * LQ + M0 - P0 + c * M_U
                    for u in us:
                        acts = h if u < 4 or u == 8 else (u_hi, u_lo)
                        wait_u = lambda k: pe.wait_ge(u_ready, (l * CH + c) * 8 + k + 1)
                        unit(n + u, q + u, u % 2, acts, KT, wait_u if u == 4 else ready, behind)

                mlp(0, (0,), lambda k: pe.wait_ge(h_ready, l * 2 * KT + KT + k + 1),
                    (lambda: mean(2 * l + 1), lambda: spread(2 * l + 1)))
                with pe.Fori(0, CH - 1) as c:
                    mlp(c, range(1, 9))
                mlp(CH - 1, range(1, 8))
            mean(2 * DEPTH)
            for b in range(TB):
                if b == 0:
                    pe.wait_ge(f_done, KT)
                if b >= 2:
                    pe.wait_ge(f_staged, b - 1)
                for k in range(KT):
                    mm = nc.tensor.transpose((sc, pt)[b % 2][:, k * P:(k + 1) * P], x[:, k, b * P:(b + 1) * P], ident[:])
                mm.then_inc(f_turned, 1)


def constants(S, D):
    import numpy as np

    f = np.float32
    pos = np.arange(S, dtype=f)

    def tables(half, base):
        inv = (f(1.0) / (f(base) ** (np.arange(half, dtype=f) / f(half)))).astype(f)
        ang = (pos[None, :] * inv[:, None]).astype(f)
        return np.cos(ang).astype(f), np.sin(ang).astype(f)

    cosA, sinA = np.ones((P, S), f), np.zeros((P, S), f)
    c, s = tables(8, 500000.0)
    for h in (0, 64):
        cosA[h:h + 8], cosA[h + 8:h + 16] = c, c
        sinA[h:h + 8], sinA[h + 8:h + 16] = -s, s
    c, s = tables(64, 10000.0)
    cosR, sinR = np.concatenate([c, c]), np.concatenate([-s, s])

    lg = np.log1p(-(f(2.0) ** (f(-5.0) - np.arange(4, dtype=f)))).astype(f)
    diff = (np.arange(S)[None, :] - np.arange(P)[:, None]).astype(f)
    decay = np.exp(np.maximum(diff, f(0))[:, None, :] * lg[None, :, None])
    decay = (np.where(diff[:, None, :] >= 0, decay, f(0)) * f(P ** -0.5)).astype(f)

    token = np.array([4 * m + r for r in range(4) for m in range(S // 4)])
    mask = np.empty((P, 4, S + 2 * P), f)
    for r in range(4):
        tq = token[r * P:(r + 1) * P]
        d1 = tq[:, None] - token[None, :]
        d2 = tq[:, None] - tq[None, :]
        mask[:, r, 0:S] = np.where((d1 >= 0) & (d1 <= 128), 0, -1e30)
        mask[:, r, S:S + P] = np.where(d2 >= 0, 0, -1e30)
        mask[:, r, S + P:] = np.where((d2 >= 0) & (d2 % 16 == 0), 0, -1e30)
    tables = np.stack([cosA, sinA, cosR, sinR], axis=1).astype(f)
    return {"tables": tables, "decay": np.ascontiguousarray(decay.transpose(1, 0, 2)),
            "mask": mask, "ident": np.eye(P, dtype=f)}


_INS = ["x", "w_in", "w_a", "w_b", "w_o", "w_up", "w_down"]


def kernel(**inputs):
    import numpy as np
    import concourse.bacc as bacc
    from concourse.bass_utils import run_bass_kernel_spmd

    nc = bacc.Bacc("TRN2", target_bir_lowering=False, num_devices=1)
    arrays = {n: np.ascontiguousarray(inputs[n]) for n in _INS}
    shape = arrays["x"].shape
    norms = [g for pair in zip(inputs["mix_norm"], inputs["ffn_norm"]) for g in pair] + [inputs["final_norm"]]
    gains = np.stack([np.asarray(g) for g in norms]).reshape(len(norms), -1, P)
    arrays["gains"] = np.ascontiguousarray(gains.transpose(2, 0, 1))
    arrays.update(constants(shape[1], shape[2]))
    feeds, aps = {}, {}
    for name, v in arrays.items():
        feeds[f"in_{name}"] = v
        aps[name] = nc.dram_tensor(f"in_{name}", v.shape, mybir.dt.from_np(v.dtype), kind="ExternalInput").ap()
    aps["out"] = nc.dram_tensor("out_x", shape, F32, kind="ExternalOutput").ap()
    trunk(nc, aps)
    r = run_bass_kernel_spmd(nc, [feeds], core_ids=[0])
    return r.results[0]["out_x"]
```

```python
from contextlib import ExitStack

import concourse.bass as bass
from concourse import mybir

P = 128
F32 = mybir.dt.float32
F32R = mybir.dt.float32r
BF16 = mybir.dt.bfloat16
ALU = mybir.AluOpType
ACT = mybir.ActivationFunctionType

EPS = 1e-6
HALVES = (slice(0, 1024), slice(1024, 2048))
SHUFFLE = [(i + 8 if i < 8 else i - 8) if i < 16 else i for i in range(32)]

UNIT_CREDIT = 4
MM_CREDIT = 4
BANK_CREDIT = 1


def trunk(nc, a):
    S = a["x"].shape[1]
    D = a["x"].shape[2]
    DEPTH = a["w_in"].shape[0]
    KT = D // P
    TB = S // P
    FF = a["w_up"].shape[2]
    GROUPS, PAIRS = 3, 4
    DH = 64
    A_W = GROUPS * PAIRS * P
    HEADS = 2 * PAIRS
    RH, RV = 4, 256
    AW = PAIRS * P
    KA = AW // P
    CH = FF // D
    COL_QR = 3 * A_W
    COL_VR = COL_QR + 2 * RH * P
    COL_GR = COL_VR + RH * RV
    COL_GA = COL_GR + RH * RV
    COL_GB = COL_GA + D

    V_U, P_U, G_U, O_U, M_U = 2, 6, 4, 2, 8
    V0 = 0
    P0 = V0 + GROUPS * V_U
    G0 = P0 + PAIRS * P_U
    O0 = G0 + 4 * G_U
    M0 = O0 + 2 * O_U
    LU = M0 + CH * M_U
    LQ = LU - P0

    with ExitStack() as ctx:
        def sb(name, shape, dt):
            return ctx.enter_context(nc.sbuf_tensor(name, shape, dt))

        def ps(name, cols):
            return ctx.enter_context(nc.psum_tensor(name, [P, cols], F32))

        def sem(name):
            return ctx.enter_context(nc.semaphore(name))

        x = sb("x", [P, KT, S], F32)
        h_hi = sb("h_hi", [P, KT, S], F32R)
        h_lo = sb("h_lo", [P, KT, S], F32R)
        raw = [sb(f"w_raw{i}", [P, 2048], F32) for i in range(2)]
        w_hi = [sb(f"w_hi{i}", [P, 2048], F32R) for i in range(2)]
        w_lo = [sb(f"w_lo{i}", [P, 2048], F32R) for i in range(2)]
        tables = sb("tables", [P, 4, S], F32)
        cosA, sinA, cosR, sinR = (tables[:, i, :] for i in range(4))
        rstd_all = sb("rstd_all", [P, S], F32)
        decay = sb("decay", [P, S], F32)
        mask = sb("mask", [P, S], F32)
        ident = sb("ident", [P, P], F32)
        ones = sb("ones", [P, P], F32)
        inv_d = sb("inv_d", [P, 1], F32)
        gains = sb("gains", [P, 2 * DEPTH + 1, KT], F32)
        gain = sb("gain", [P, 2, KT], F32)
        std = sb("std", [P, 2 * TB], F32)
        rstd = sb("rstd", [P, 2 * TB], F32)
        eps = sb("eps", [P, 1], F32)
        stats = sb("stats", [P, 2 * TB, 2, HEADS], F32)
        other = sb("other", [P, 2 * TB, 2, HEADS], F32)
        tick = sb("tick", [P, 1], F32)
        warm = sb("warm", [P, 1], F32)

        zone0 = -(-nc.sbuf_base // 64) * 64
        top = {}

        def at(scope, name, shape, dt):
            off = top.get(scope, zone0)
            n = 2 if dt == BF16 else 4
            for d in shape[1:]:
                n *= d
            top[scope] = off + -(-n // 32) * 32
            return nc.alloc_sbuf_tensor_at(name, shape, dt, offset=off)

        z = at("P", "z", [P, KT, S], F32)
        U = at("P", "U", [P, 2, TB, AW], F32)
        vA = at("P", "vA", [P, TB, A_W], F32)
        qk = at("P", "qk", [P, 2 * GROUPS, S], F32)
        qkR = at("P", "qkR", [P, 2, S], F32)
        vR = at("P", "vR", [P, TB, RV], F32)
        ST = at("P", "ST", [P, sum(range(1, TB + 1)) * P], F32)
        prob = at("P", "prob", [P, S], F32)
        probT = at("P", "probT", [P, S], F32)
        rot = at("P", "rot", [P, S], F32)
        swp = at("P", "swp", [P, S], F32)
        rcos = at("P", "rcos", [P, S], F32)
        silu = at("P", "silu", [P, 2, S], F32)
        nmax = at("P", "nmax", [P, 2 * TB, 2], F32)
        den = at("P", "den", [P, 2 * TB, 2], F32)
        m_hi = at("G", "m_hi", [P, KT, S], F32R)
        m_lo = at("G", "m_lo", [P, KT, S], F32R)
        z_hi = at("G", "z_hi", [P, KT, S], F32R)
        z_lo = at("G", "z_lo", [P, KT, S], F32R)
        pad = top["G"]
        y_hi = at("G", "y_hi", [P, KA, S], F32R)
        y_lo = at("G", "y_lo", [P, KA, S], F32R)
        sA = at("G", "sA", [P, 2, S], F32)
        sB = at("G", "sB", [P, 2, S], F32)
        y_sum = at("G", "y_sum", [P, 2, S], F32)
        fac = [at("G", f"fac{i}", [P, 2 * TB, HEADS], F32) for i in range(5)]
        u_hi, u_lo = z_hi, z_lo
        top["N"] = pad
        ssum = at("N", "ssum", [P, S], F32)
        sq = at("N", "sq", [P, 2, S], F32)
        diag = at("N", "diag", [P, TB, P], F32)
        hn = at("N", "hn", [P, 2, S], F32)
        relu = at("N", "relu", [P, 2, S], F32)
        relu2 = at("N", "relu2", [P, 2, S], F32)
        gdiag = at("N", "gdiag", [P, KT, P], F32)
        x_nat = at("X", "x_nat", [P, TB, D], F32)
        stage = at("Y", "stage", [P, TB, D], F32)
        for k_, v_ in top.items():
            assert v_ <= nc.sbuf_usable_end, (k_, v_, nc.sbuf_usable_end)

        pj = [ps(f"pj{i}", S) for i in range(2)]
        sc = ps("sc", 2 * S)
        pt = ps("pt", S)
        yo = ps("yo", 2 * S)
        rb = ps("rb", S)
        xbank = [sc[:, 0:S], sc[:, S:2 * S], pt[:], yo[:, 0:S], yo[:, S:2 * S], rb[:], pj[0][:], pj[1][:]]
        fbank = [xbank[0:2], xbank[3:5], xbank[6:8], xbank[0:2]]
        ybank = [xbank[3:5], xbank[0:2]]
        vbank = [sc[:, 0:S], sc[:, S:2 * S], pt[:], yo[:, 0:S]]

        gains_in = sem("gains_in")
        mask_in = sem("mask_in")
        ident_in = sem("ident_in")
        tables_in = sem("tables_in")
        tables_done = sem("tables_done")
        const_set = sem("const_set")
        x_in = [sem(f"x_in{i}") for i in range(2)]
        x_turned = sem("x_turned")
        x_init = sem("x_init")
        gain_set = sem("gain_set")
        landed = [sem(f"landed{i}") for i in range(2)]
        hi_done = sem("hi_done")
        lo_done = sem("lo_done")
        mm_done = sem("mm_done")
        bank_free = [sem(f"bank_free{i}") for i in range(2)]
        sq_done = sem("sq_done")
        sum_done = sem("sum_done")
        mean_done = sem("mean_done")
        std_done = sem("std_done")
        rstd_done = sem("rstd_done")
        diag_done = sem("diag_done")
        spread_done = sem("spread_done")
        rstd_all_done = sem("rstd_all_done")
        hn_done = sem("hn_done")
        h_hi_done = sem("h_hi_done")
        h_ready = sem("h_ready")
        v_done = sem("v_done")
        v_out = sem("v_out")
        rot_swap = sem("rot_swap")
        rot_sin = sem("rot_sin")
        rot_cos = sem("rot_cos")
        rot_out = sem("rot_out")
        att_qk = sem("att_qk")
        att_masked = sem("att_masked")
        att_exp = sem("att_exp")
        att_turned = sem("att_turned")
        att_probT = sem("att_probT")
        att_pv = sem("att_pv")
        u_out = sem("u_out")
        stats_done = sem("stats_done")
        stats_sent = sem("stats_sent")
        other_in = sem("other_in")
        fac_diff = sem("fac_diff")
        fac_exp = sem("fac_exp")
        fac_step = sem("fac_step")
        u_scaled = sem("u_scaled")
        y_turned = sem("y_turned")
        y_copied = sem("y_copied")
        y_summed = sem("y_summed")
        y_hi_done = sem("y_hi_done")
        y_ready = sem("y_ready")
        decay_in = sem("decay_in")
        st_mm = sem("st_mm")
        st_out = sem("st_out")
        ret_mm = sem("ret_mm")
        ret_sq = sem("ret_sq")
        ret_out = sem("ret_out")
        ret_sum = sem("ret_sum")
        ret_mean = sem("ret_mean")
        ret_std = sem("ret_std")
        ret_rstd = sem("ret_rstd")
        ret_scaled = sem("ret_scaled")
        z_done = sem("z_done")
        g_sigmoid = sem("g_sigmoid")
        silu_done = sem("silu_done")
        gate_sigmoid = sem("gate_sigmoid")
        relu_scaled = sem("relu_scaled")
        split_hi = sem("split_hi")
        split_done = sem("split_done")
        merged = sem("merged")
        m_hi_done = sem("m_hi_done")
        m_ready = sem("m_ready")
        relu2_done = sem("relu2_done")
        u_hi_done = sem("u_hi_done")
        u_ready = sem("u_ready")
        gdiag_done = sem("gdiag_done")
        f_turned = sem("f_turned")
        f_staged = [sem(f"f_staged{i}") for i in range(2)]
        out_done = sem("out_done")

        st0 = [sum(S - P * i for i in range(j)) for j in range(TB)]

        def keys(side, b):
            return slice(2 * P, 4 * P) if side else slice(0 if b >= 2 else P, 2 * P)

        def by_residue(v):
            return v.rearrange("p (m r) -> p r m", r=4)

        block = ctx.enter_context(nc.Block())

        w_in_t = a["w_in"].rearrange("l (k p) (t c) -> l p k t c", p=P, c=P)
        w_in_u = a["w_in"].rearrange("l (k p) (t c) -> l p k t c", p=P, c=2 * P)
        w_in_v = a["w_in"].rearrange("l (k p) (t c) -> l p k t c", p=P, c=4 * P)
        w_a_u = a["w_a"].rearrange("l (k p) (t c) -> l p k t c", p=P, c=2 * P)
        w_b_u = a["w_b"].rearrange("l (k p) (t c) -> l p k t c", p=P, c=2 * P)
        w_o_u = a["w_o"].rearrange("l (k p) (t c) -> l p k t c", p=P, c=2 * P)
        w_up_u = a["w_up"].rearrange("l (k p) (t c) -> l p k t c", p=P, c=2 * P)
        w_down_u = a["w_down"].rearrange("l (f k p) (t c) -> l p f k t c", p=P, k=KT, c=2 * P)

        scratch = nc.dram_tensor("stats_scratch", [2, S, 2 * HEADS], F32, kind="Internal").ap()

        @block.sync
        def _(sp):
            sp.dma_start(ident[:], a["ident"]).then_inc(ident_in, 16)
            for i in range(2):
                c = slice(i * D // 2, (i + 1) * D // 2)
                sp.dma_start(x_nat[:, :, c], a["x"].rearrange("b (t p) d -> p (b t) d", p=P)[:, :, c]).then_inc(x_in[i], 16)

            def load(n, s, halves):
                sp.wait_ge(lo_done, (n - 1) * 2 + UNIT_CREDIT)
                for dst, src in halves:
                    sp.dma_start(dst, src).then_inc(landed[s], 16)

            def tiles(s, v, t0, t1):
                d = raw[s][:].rearrange("p (k o c) -> p k o c", o=2, c=P)
                return [(d[:, :, 0, :], v[:, :, t0, :]), (d[:, :, 1, :], v[:, :, t1, :])]

            def cols(s, v, t, kt=KT):
                d = raw[s][:].rearrange("p (k c) -> p k c", k=KT)
                m = kt // 2
                return [(d[:, 0:m, :], v[:, 0:m, t, :]), (d[:, m:kt, :], v[:, m:kt, t, :])]

            with sp.Fori(0, DEPTH) as l:
                with sp.Fori(0, GROUPS) as g:
                    for u in range(V_U):
                        d = raw[u][:].rearrange("p (k c) -> p k c", k=4)
                        load(l * LU + V0 + g * V_U + u, u,
                             [(d[:, m:m + 2, :], w_in_v[l, :, 4 * u + m:4 * u + m + 2, 2 * GROUPS + g, :])
                              for m in (0, 2)])
                sp.wait_ge(rot_out, l * 8 * PAIRS + 1)
                sp.dma_start(tables[:], a["tables"]).then_inc(tables_in, 16)
                with sp.Fori(0, PAIRS) as i:
                    n = l * LU + P0 + i * P_U
                    for g in range(GROUPS):
                        load(n + g, g % 2, tiles(g % 2, w_in_t[l], PAIRS * g + i, PAIRS * (GROUPS + g) + i))
                    load(n + 3, 1, tiles(1, w_in_t[l], COL_QR // P + i, COL_QR // P + RH + i))
                    load(n + 4, 0, cols(0, w_in_u[l], COL_VR // 256 + i))
                    sp.wait_ge(st_out, (l * PAIRS + i) * TB + 1)
                    sp.dma_start(decay[:], a["decay"][i]).then_inc(decay_in, 16)
                    load(n + 5, 1, cols(1, w_in_u[l], COL_GR // 256 + i))
                def gates(p, exchange=None):
                    n = l * LU + G0 + p * G_U
                    load(n + 0, 0, cols(0, w_in_u[l], COL_GA // 256 + p))
                    load(n + 1, 1, cols(1, w_in_u[l], COL_GB // 256 + p))
                    load(n + 2, 0, cols(0, w_b_u[l], p))
                    if exchange:
                        exchange()
                    load(n + 3, 1, cols(1, w_a_u[l], p, KA))

                def exchange():
                    sp.wait_ge(stats_done, (l + 1) * 2 * PAIRS)
                    in_order = lambda v: v.rearrange("(b p) c -> p b c", p=P)
                    residues = lambda v: v.rearrange("(p r) c -> p r c", r=TB)
                    for side, view in enumerate((in_order, residues)):
                        st = slice(side * TB, (side + 1) * TB)
                        sp.dma_start(view(scratch[side]),
                                     stats[:, st].rearrange("p b w h -> p b (w h)")).then_inc(stats_sent, 16)
                    sp.wait_ge(stats_sent, l * 32 + 32)
                    for side, view in enumerate((in_order, residues)):
                        st = slice(side * TB, (side + 1) * TB)
                        sp.dma_start(other[:, st].rearrange("p b w h -> p b (w h)"),
                                     view(scratch[1 - side])).then_inc(other_in, 16)

                gates(0, exchange)
                with sp.Fori(1, 4) as p:
                    gates(p)
                with sp.Fori(0, 2) as i:
                    for u in range(O_U):
                        load(l * LU + O0 + i * O_U + u, u, cols(u, w_o_u[l], 2 * i + u))
                with sp.Fori(0, CH) as c:
                    n = l * LU + M0 + c * M_U
                    for u in range(4):
                        load(n + u, u % 2, cols(u % 2, w_up_u[l], 4 * c + u))
                    for u in range(4):
                        load(n + 4 + u, u % 2, cols(u % 2, w_down_u[l, :, c], u))
            sp.wait_ge(lo_done, (DEPTH * LU - 1) * 2 + UNIT_CREDIT)
            sp.sem_inc(landed[0], 32)

            out_v = a["out"].rearrange("b (t p) d -> (b t) p d", p=P)
            for b in range(TB):
                for i in range(2):
                    c = slice(i * S, (i + 1) * S)
                    sp.wait_ge(f_staged[i], b + 1)
                    sp.dma_start(out_v[b][:, c], stage[:, b, c]).then_inc(out_done, 16)
            sp.wait_ge(out_done, 16 * 2 * TB)

        @block.scalar
        def _(act):
            act.wait_ge(const_set, 3)
            nc.scalar.dma_start(gains[:], a["gains"]).then_inc(gains_in, 16)
            nc.scalar.copy(warm[:], eps[:])

            def hi_halves(s):
                for c in HALVES:
                    nc.scalar.copy(w_hi[s][:, c], raw[s][:, c]).then_inc(hi_done, 1)

            def split_unit(half, n, s):
                act.wait_ge(landed[s], half * 32 + 32)
                act.wait_ge(mm_done, n * 2 - 2 + MM_CREDIT)
                hi_halves(s)

            def ahead(l, base, per, i, u):
                k = u + 1
                split_unit(l * (LU // 2) + base // 2 + i * (per // 2) + k // 2, l * LU + base + i * per + k, k % 2)

            def banks(l, base, per, i, u):
                return l * LQ + base - P0 + i * per + u

            def square_and_split(J, k):
                if k >= 2:
                    act.wait_ge(sum_done, J * (KT - 1) + max(k - 2, 1))
                nc.scalar.activation(sq[:, k % 2, :], x[:, k, :], ACT.Square).then_inc(sq_done, 1)
                act.wait_ge(hn_done, J * KT + k + 1)
                nc.scalar.copy(h_hi[:, k, :], hn[:, k % 2, :]).then_inc(h_hi_done, 1)

            def rms(J):
                act.wait_ge(mean_done, J + 1)
                nc.scalar.activation(std[:], rb[:, 0:2 * TB], ACT.Sqrt, bias=eps[:]).then_inc(std_done, 1)

            def x_copy(k):
                act.wait_ge(x_turned, k + 1)
                nc.scalar.copy(x[:, k, :], xbank[k]).then_inc(x_init, 1)

            def x_split(k):
                act.wait_ge(x_init, k + 1)
                square_and_split(0, k)

            x_copy(0)
            x_copy(1)
            x_split(0)
            x_copy(2)
            x_copy(3)
            x_split(1)
            act.wait_ge(landed[0], 32)
            hi_halves(0)
            nc.scalar.dma_start(mask[:], a["mask"]).then_inc(mask_in, 16)
            for k in range(2, KT):
                x_split(k)
                if k + 2 < KT:
                    x_copy(k + 2)

            with act.Fori(0, DEPTH) as l:
                ahead(l, V0, V_U, 0, 0)
                rms(2 * l)
                with act.Fori(0, GROUPS - 1) as g:
                    ahead(l, V0, V_U, g, 1)
                    ahead(l, V0, V_U, g, 2)
                ahead(l, V0, V_U, GROUPS - 1, 1)
                with act.Fori(0, PAIRS) as i:
                    J = l * PAIRS + i
                    n = l * LU + P0 + i * P_U
                    q = banks(l, P0, P_U, i, 0)

                    def tile(u, o):
                        act.wait_ge(mm_done, (n + u) * 2 + o + 1 + MM_CREDIT)

                    def rot_in(u, o):
                        t = 2 * u + o
                        tile(u, o)
                        act.wait_ge(rot_out, J * 8 + t + 1)
                        if u < GROUPS:
                            nc.scalar.copy(rot[:], pj[o][:]).then_inc(bank_free[o], 1)
                        else:
                            nc.scalar.copy(rot[:], pj[o][:])
                            nc.scalar.copy(swp[0:64, :], pj[o][64:128, :])
                            nc.scalar.copy(swp[64:128, :], pj[o][0:64, :]).then_inc(bank_free[o], 1)

                    def exp(b):
                        for side in range(2):
                            act.wait_ge(att_masked, (J * 8 + b) * 2 + side + 1)
                            c, at_ = keys(side, b), side * TB + b // 2
                            nc.scalar.activation(prob[:, c], prob[:, c], ACT.Exp, scale=-1.0,
                                                 bias=nmax[:, at_, b % 2:b % 2 + 1],
                                                 accum_out=den[:, at_, b % 2:b % 2 + 1]).then_inc(att_exp, 1)

                    def probT_out(b):
                        act.wait_ge(att_turned, J * 8 + b + 1)
                        if b >= 1:
                            act.wait_ge(att_pv, J * 8 + b)
                        c = slice(keys(0, b).start, S)
                        nc.scalar.copy(probT[:, c], pt[:, c]).then_inc(att_probT, 1)

                    for u in range(GROUPS):
                        ahead(l, P0, P_U, i, u)
                        rot_in(u, 0)
                        rot_in(u, 1)
                    ahead(l, P0, P_U, i, 3)
                    exp(0)
                    rot_in(3, 0)
                    probT_out(0)
                    exp(1)
                    probT_out(1)
                    exp(2)
                    ahead(l, P0, P_U, i, 4)
                    rot_in(3, 1)
                    probT_out(2)
                    exp(3)
                    probT_out(3)
                    exp(4)

                    def vR_out(o):
                        tile(4, o)
                        if o == 0:
                            act.wait_ge(ret_mm, J * 2 + 1 + 1)
                        for half in range(2):
                            b = 2 * o + half
                            mm = nc.scalar.activation(vR[:, b, :], pj[o][:, half * RV:(half + 1) * RV], ACT.Copy,
                                                      scale=rstd[:, b:b + 1])
                        mm.then_inc(bank_free[o], 1)

                    vR_out(0)
                    probT_out(4)
                    exp(5)
                    probT_out(5)
                    exp(6)
                    ahead(l, P0, P_U, i, 5)
                    vR_out(1)
                    probT_out(6)
                    exp(7)
                    probT_out(7)

                    def ret_square(e):
                        act.wait_ge(ret_out, J * 2 + e + 1)
                        nc.scalar.activation(sqR[e], rb[:],
                                             ACT.Square).then_inc(ret_sq, 1)

                    def gate_sig(o):
                        act.wait_ge(bank_free[o], q + 6 + BANK_CREDIT)
                        nc.scalar.activation(sigR[o], silu[:, o, :], ACT.Sigmoid).then_inc(g_sigmoid, 1)

                    sigR = [swp[:], prob[:, 0:S]]
                    sqR = [rot[:], probT[:, 0:S]]
                    ret_square(0)
                    gate_sig(0)
                    act.wait_ge(att_pv, J * 8 + 8)
                    ret_square(1)
                    gate_sig(1)
                    act.wait_ge(ret_mean, J + 1)
                    nc.scalar.activation(probT[:], rb[:], ACT.Sqrt, bias=eps[:], scale=1.0 / RV).then_inc(ret_std, 1)
                def split_z(ks):
                    for k in ks:
                        nc.scalar.copy(z_hi[:, k, :], z[:, k, :]).then_inc(split_hi, 1)

                def gate(p, u, o):
                    act.wait_ge(bank_free[o], l * LQ + G0 - P0 + p * G_U + u + 1 + BANK_CREDIT)
                    dst = (sA, sB)[u]
                    nc.scalar.activation(dst[:, o, :], dst[:, o, :], ACT.Sigmoid).then_inc(gate_sigmoid, 1)

                ahead(l, G0, G_U, 0, 0)
                def y_copy(j):
                    act.wait_ge(y_turned, l * PAIRS + j + 1)
                    if j >= 2:
                        act.wait_ge(y_ready, l * PAIRS + j - 1)
                    nc.scalar.copy(y_sum[:, j % 2, :], ybank[j % 2][0]).then_inc(y_copied, 1)

                def y_split(j):
                    act.wait_ge(y_summed, l * PAIRS + j + 1)
                    nc.scalar.copy(y_hi[:, j, :], y_sum[:, j % 2, :]).then_inc(y_hi_done, 1)

                for i in (1, 2):
                    act.wait_ge(fac_diff, l * 3 + i + 1)
                    nc.scalar.activation(fac[i][:], fac[i][:], ACT.Exp).then_inc(fac_exp, 1)
                gate(0, 0, 0)
                act.wait_ge(z_done, l * KT + KT)
                split_z(range(0, 4))
                gate(0, 0, 1)
                ahead(l, G0, G_U, 0, 1)
                split_z(range(4, 8))
                gate(0, 1, 0)
                gate(0, 1, 1)
                y_copy(0)
                y_copy(1)
                y_split(0)
                y_split(1)
                ahead(l, G0, G_U, 0, 2)
                y_copy(2)
                y_copy(3)
                y_split(2)
                y_split(3)
                with act.Fori(0, 3) as p:
                    ahead(l, G0, G_U, p, 3)
                    for u in range(2):
                        ahead(l, G0, G_U, p, 4 + u)
                        for o in range(2):
                            gate(p + 1, u, o)
                    ahead(l, G0, G_U, p, 6)
                ahead(l, G0, G_U, 3, 3)
                def added(u, o, count):
                    act.wait_ge(bank_free[o], count + BANK_CREDIT)

                for u in range(4):
                    ahead(l, O0, O_U, 0, u)
                    for o in range(2):
                        added(u, o, l * LQ + O0 - P0 + u + 1)
                        square_and_split(2 * l + 1, 2 * u + o)
                def relu_out(c, u, o):
                    act.wait_ge(mm_done, (l * LU + M0 + c * M_U + u) * 2 + o + 1 + MM_CREDIT)
                    nc.scalar.activation(relu[:, o, :], pj[o][:], ACT.Relu).then_inc(bank_free[o], 1)

                def u_split(c, u, o):
                    t = 2 * u + o if u < 8 else 8 + o
                    act.wait_ge(relu2_done, (l * CH + c) * 8 + t + 1)
                    nc.scalar.copy(u_hi[:, t % 8, :], relu2[:, o, :]).then_inc(u_hi_done, 1)

                def up(c, u):
                    ahead(l, M0, M_U, c, u)
                    for o in range(2):
                        relu_out(c, u, o)
                        u_split(c, u, o)

                ahead(l, M0, M_U, 0, 0)
                relu_out(0, 0, 0)
                rms(2 * l + 1)
                relu_out(0, 0, 1)
                u_split(0, 0, 0)
                u_split(0, 0, 1)
                with act.Fori(0, CH - 1) as c:
                    for u in (1, 2, 3):
                        up(c, u)
                    for u in (4, 5, 6, 7):
                        ahead(l, M0, M_U, c, u)
                    up(c, 8)
                for u in (1, 2, 3):
                    up(CH - 1, u)
                for u in (4, 5, 6, 7):
                    ahead(l, M0, M_U, CH - 1, u)
                    for o in range(2):
                        added(u, o, l * LQ + M0 - P0 + (CH - 1) * M_U + u + 1)
                        square_and_split(2 * l + 2, 2 * (u - 4) + o)
            act.wait_ge(mean_done, 2 * DEPTH + 1)
            nc.scalar.activation(std[:, 0:TB], rb[:, 0:TB], ACT.Sqrt, bias=eps[:]).then_inc(std_done, 1)
            act.wait_ge(rstd_done, 2 * DEPTH + 1)
            for b in range(TB):
                act.wait_ge(f_turned, b + 1)
                nc.scalar.activation(stage[:, b, 0:S], fbank[b][0], ACT.Copy,
                                     scale=rstd[:, b:b + 1]).then_inc(f_staged[0], 1)

        @block.gpsimd
        def _(pool):
            nc.gpsimd.memset(ones[:], 1.0).then_inc(const_set, 1)
            nc.gpsimd.memset(inv_d[:], 1.0 / D).then_inc(const_set, 1)
            nc.gpsimd.memset(eps[:], EPS).then_inc(const_set, 1)
            pool.sem_inc(lo_done, UNIT_CREDIT)

            def lo(n, s, halves=(0, 1)):
                for i in halves:
                    c = HALVES[i]
                    pool.wait_ge(hi_done, n * 2 + i + 1)
                    nc.gpsimd.tensor_tensor(w_lo[s][:, c], raw[s][:, c], w_hi[s][:, c],
                                            ALU.subtract).then_inc(lo_done, 1)

            pool.wait_ge(lo_done, 1 + UNIT_CREDIT)
            lo(0, 0, (1,))
            with pool.Fori(0, DEPTH) as l:
                with pool.Fori(0, GROUPS) as g:
                    for u in range(V_U):
                        lo(l * LU + V0 + g * V_U + u + 1, (u + 1) % 2)
                with pool.Fori(0, PAIRS) as i:
                    J = l * PAIRS + i
                    n = l * LU + P0 + i * P_U
                    q = l * LQ + i * P_U
                    for u in range(P_U):
                        lo(n + u + 1, (u + 1) % 2)
                        for o in range(2 if u < 4 else 0):
                            pool.wait_ge(bank_free[o], q + u + 1 + BANK_CREDIT)
                            pool.wait_ge(rot_out, J * 8 + 2 * u + o + 1)
                            pool.wait_ge(tables_done, l + 1)
                            nc.gpsimd.tensor_tensor(rcos[:], rot[:], cosA if u < 3 else cosR,
                                                    ALU.mult).then_inc(rot_cos, 1)
                with pool.Fori(0, (LU - G0) // 2) as j:
                    for u in range(2):
                        lo(l * LU + G0 + 2 * j + u + 1, (u + 1) % 2)

        @block.vector
        def _(dve):
            for s in bank_free:
                dve.sem_inc(s, BANK_CREDIT)
            dve.sem_inc(rot_out, 1)
            dve.sem_inc(u_out, 2)
            dve.sem_inc(ret_std, 1)
            dve.sem_inc(st_out, 1)
            dve.sem_inc(v_out, TB)
            dve.sem_inc(m_ready, 2)

            def scale_and_split(J, k, g):
                if k >= 2:
                    dve.wait_ge(h_ready, J * KT + k - 1)
                nc.vector.tensor_scalar(hn[:, k % 2, :], x[:, k, :], g[:, k:k + 1], None,
                                        ALU.mult).then_inc(hn_done, 1)
                if k >= 1:
                    dve.wait_ge(sq_done, J * KT + k + 1)
                    if k > 1:
                        dve.wait_ge(sum_done, J * (KT - 1) + k - 1)
                    nc.vector.tensor_tensor(ssum[:], sq[:, 0, :] if k == 1 else ssum[:], sq[:, k % 2, :],
                                            ALU.add).then_inc(sum_done, 1)
                dve.wait_ge(h_hi_done, J * KT + k + 1)
                nc.vector.tensor_tensor(h_lo[:, k, :], hn[:, k % 2, :], h_hi[:, k, :],
                                        ALU.subtract).then_inc(h_ready, 1)

            def rms(J, squared=False):
                dve.wait_ge(std_done, J + 1)
                nc.vector.reciprocal(rstd[:], std[:]).then_inc(rstd_done, 1)
                dve.wait_ge(rstd_done, J + 1)
                for b in range(TB):
                    r = rstd[:, b:b + 1]
                    mm = nc.vector.tensor_scalar(diag[:, b, :], ident[:], r, r if squared else None, ALU.mult,
                                                 ALU.mult if squared else ALU.bypass)
                mm.then_inc(diag_done, 1)

            def rms_spread(J):
                dve.wait_ge(spread_done, J + 1)
                nc.vector.tensor_copy(rstd_all[:], rb[:]).then_inc(rstd_all_done, 1)
                dve.wait_ge(rstd_all_done, J + 1)

            dve.wait_ge(ident_in, 16)
            for k in range(KT):
                dve.wait_ge(x_init, k + 1)
                if k == 0:
                    dve.wait_ge(gains_in, 16)
                if k == 2:
                    dve.wait_ge(hi_done, 1)
                    dve.wait_ge(lo_done, UNIT_CREDIT)
                    nc.vector.tensor_tensor(w_lo[0][:, HALVES[0]], raw[0][:, HALVES[0]], w_hi[0][:, HALVES[0]],
                                            ALU.subtract).then_inc(lo_done, 1)
                scale_and_split(0, k, gains[:, 0, :])
            dve.wait_ge(mask_in, 16)

            with dve.Fori(0, DEPTH) as l:
                nc.vector.tensor_scalar(gain[:].rearrange("p w k -> p (w k)"),
                                        gains[:, bass.ds(l * 2 + 1, 2), :].rearrange("p w k -> p (w k)"), 1.0, None,
                                        ALU.mult).then_inc(gain_set, 1)
                rms(2 * l)
                for g in range(GROUPS):
                    for b in range(TB):
                        if b < TB - 1:
                            dve.wait_ge(v_done, (l * GROUPS + g) * (TB - 1) + b + 1)
                        else:
                            dve.wait_ge(mm_done, (l * LU + V0 + g * V_U + 2) * 2 + MM_CREDIT)
                        at_ = b if g == 0 else TB + b
                        nc.vector.tensor_scalar(vA[:, b, g * AW:(g + 1) * AW], vbank[b],
                                                rstd[:, at_:at_ + 1], None, ALU.mult).then_inc(v_out, 1)
                rms_spread(2 * l)
                dve.wait_ge(tables_in, l * 16 + 16)
                for i in range(4):
                    mm = nc.vector.tensor_tensor(tables[:, i, :], tables[:, i, :], rstd_all[:], ALU.mult)
                mm.then_inc(tables_done, 1)
                with dve.Fori(0, PAIRS) as i:
                    J = l * PAIRS + i
                    n = l * LU + P0 + i * P_U
                    q = l * LQ + i * P_U

                    def rotary(u, o):
                        t = 2 * u + o
                        dve.wait_ge(bank_free[o], q + u + 1 + BANK_CREDIT)
                        if t == 0:
                            dve.wait_ge(tables_done, l + 1)
                        if u < GROUPS:
                            nc.vector.memset(tick[:], 0.0)
                            nc.vector.stream_shuffle(swp[:], rot[:], SHUFFLE).then_inc(rot_swap, 1)
                            dve.wait_ge(rot_swap, J * 6 + t + 1)
                        nc.vector.tensor_tensor(swp[:], swp[:], sinA if u < GROUPS else sinR,
                                                ALU.mult).then_inc(rot_sin, 1)
                        dve.wait_ge(rot_sin, J * 8 + t + 1)
                        dve.wait_ge(rot_cos, J * 8 + t + 1)
                        if u == 0:
                            nc.vector.tensor_tensor(qk[:, t, :], rcos[:], swp[:], ALU.add).then_inc(rot_out, 1)
                        elif u < GROUPS:
                            nc.vector.tensor_tensor(qk[:, t, :].rearrange("p (r m) -> p r m", r=4),
                                                    by_residue(rcos[:]), by_residue(swp[:]),
                                                    ALU.add).then_inc(rot_out, 1)
                        else:
                            nc.vector.tensor_tensor(qkR[:, o, :], rcos[:], swp[:], ALU.add).then_inc(rot_out, 1)

                    def masked(b):
                        for side in range(2):
                            if side == 0:
                                dve.wait_ge(att_qk, J * 8 + b + 1)
                                if b >= 1:
                                    dve.wait_ge(att_turned, J * 8 + b)
                                nc.vector.memset(tick[:], 0.0)
                            c, at_ = keys(side, b), side * TB + b // 2
                            nc.vector.tensor_tensor_reduce(
                                out=prob[:, c], in0=sc[:, (b % 2) * S + c.start:(b % 2) * S + c.stop],
                                in1=mask[:, c], scale=-(DH ** -0.5), scalar=3e38, op0=ALU.add, op1=ALU.min,
                                accum_out=nmax[:, at_, b % 2:b % 2 + 1]).then_inc(att_masked, 1)

                    def u_copy():
                        dve.wait_ge(att_pv, J * 8 + 8)
                        for side in range(2):
                            nc.vector.tensor_scalar(
                                U[:, side, :, bass.ds(i * P, P)],
                                yo[:, side * S:(side + 1) * S].rearrange("p (b c) -> p b c", b=TB), 1.0, None,
                                ALU.mult).then_inc(u_out, 1)
                        for which, src in enumerate((nmax, den)):
                            nc.vector.tensor_scalar(stats[:, :, which, bass.ds(2 * i, 2)], src[:], 1.0, None,
                                                    ALU.mult).then_inc(stats_done, 1)

                    def st_decayed(j):
                        dve.wait_ge(st_mm, J * TB + j + 1)
                        w = S - j * P
                        if j == 0:
                            dve.wait_ge(decay_in, J * 16 + 16)
                        nc.vector.tensor_tensor(ST[:, st0[j]:st0[j] + w], rb[:, 0:w], decay[:, 0:w],
                                                ALU.mult).then_inc(st_out, 1)

                    def ret_copy(e):
                        dve.wait_ge(ret_mm, J * 2 + e + 1 + 2)
                        nc.vector.tensor_scalar(z[:, bass.ds(2 * i + e, 1), :].rearrange("p k s -> p (k s)"),
                                                rb[:], 1.0, None, ALU.mult).then_inc(ret_out, 1)

                    def gate_scale(o):
                        dve.wait_ge(mm_done, (n + 5) * 2 + o + 1 + MM_CREDIT)
                        nc.vector.tensor_tensor(silu[:, o, :], pj[o][:], rstd_all[:], ALU.mult).then_inc(bank_free[o], 1)

                    def silu_gate(o):
                        dve.wait_ge(g_sigmoid, J * 2 + o + 1)
                        nc.vector.tensor_tensor(silu[:, o, :], silu[:, o, :], (swp[:], prob[:, 0:S])[o],
                                                ALU.mult).then_inc(silu_done, 1)

                    for t in range(6):
                        rotary(t // 2, t % 2)
                    masked(0)
                    rotary(3, 0)
                    masked(1)
                    masked(2)
                    masked(3)
                    rotary(3, 1)
                    for s in range(4):
                        masked(4 + s)
                        st_decayed(s)
                    ret_copy(0)
                    u_copy()
                    gate_scale(0)
                    ret_copy(1)
                    silu_gate(0)
                    dve.wait_ge(ret_sq, J * 2 + 2)
                    nc.vector.tensor_tensor(rcos[:], probT[:, 0:S], rot[:], ALU.add).then_inc(ret_sum, 1)
                    gate_scale(1)
                    silu_gate(1)
                    dve.wait_ge(ret_std, J + 1 + 1)
                    nc.vector.reciprocal(probT[:, 0:S], probT[:, 0:S]).then_inc(ret_rstd, 1)
                    dve.wait_ge(ret_rstd, J + 1)
                    for e in range(2):
                        ze = z[:, bass.ds(2 * i + e, 1), :].rearrange("p k s -> p (k s)")
                        dve.wait_ge(silu_done, J * 2 + e + 1)
                        nc.vector.tensor_tensor(silu[:, e, :], silu[:, e, :], probT[:, 0:S],
                                                ALU.mult).then_inc(ret_scaled, 1)
                        dve.wait_ge(ret_scaled, J * 2 + e + 1)
                        nc.vector.tensor_tensor(ze, ze, silu[:, e, :], ALU.mult).then_inc(z_done, 1)
                def split_z(ks):
                    for k in ks:
                        dve.wait_ge(split_hi, l * KT + k + 1)
                        nc.vector.tensor_tensor(z_lo[:, k, :], z[:, k, :], z_hi[:, k, :],
                                                ALU.subtract).then_inc(split_done, 1)

                def y_add(j):
                    dve.wait_ge(y_copied, l * PAIRS + j + 1)
                    nc.vector.tensor_tensor(y_sum[:, j % 2, :], ybank[j % 2][1], y_sum[:, j % 2, :], ALU.add).then_inc(y_summed, 1)

                def y_split(j):
                    dve.wait_ge(y_hi_done, l * PAIRS + j + 1)
                    nc.vector.tensor_tensor(y_lo[:, j, :], y_sum[:, j % 2, :], y_hi[:, j, :],
                                            ALU.subtract).then_inc(y_ready, 1)

                def factors():
                    nm, d, nm_, d_ = stats[:, :, 0, :], stats[:, :, 1, :], other[:, :, 0, :], other[:, :, 1, :]
                    dve.wait_ge(other_in, l * 32 + 32)
                    nc.vector.tensor_tensor(fac[0][:], nm, nm_, ALU.min).then_inc(fac_diff, 1)
                    dve.wait_ge(fac_diff, l * 3 + 1)
                    nc.vector.tensor_tensor(fac[1][:], fac[0][:], nm, ALU.subtract).then_inc(fac_diff, 1)
                    nc.vector.tensor_tensor(fac[2][:], fac[0][:], nm_, ALU.subtract).then_inc(fac_diff, 1)
                    dve.wait_ge(fac_exp, l * 2 + 2)
                    nc.vector.tensor_tensor(fac[3][:], fac[1][:], d, ALU.mult).then_inc(fac_step, 1)
                    nc.vector.tensor_tensor(fac[4][:], fac[2][:], d_, ALU.mult).then_inc(fac_step, 1)
                    dve.wait_ge(fac_step, l * 5 + 2)
                    nc.vector.tensor_tensor(fac[3][:], fac[3][:], fac[4][:], ALU.add).then_inc(fac_step, 1)
                    dve.wait_ge(fac_step, l * 5 + 3)
                    nc.vector.reciprocal(fac[3][:], fac[3][:]).then_inc(fac_step, 1)
                    dve.wait_ge(fac_step, l * 5 + 4)
                    nc.vector.tensor_tensor(fac[0][:], fac[1][:], fac[3][:], ALU.mult).then_inc(fac_step, 1)
                    dve.wait_ge(fac_step, l * 5 + 5)

                def u_scale(j):
                    for side in range(2):
                        u = U[:, side, :, j * P:(j + 1) * P].rearrange("p b (h d) -> p b h d", h=2)
                        f = fac[0][:, side * TB:(side + 1) * TB, 2 * j:2 * j + 2]
                        nc.vector.tensor_tensor(u, u, f.unsqueeze(3).to_broadcast([P, TB, 2, DH]),
                                                ALU.mult).then_inc(u_scaled, 1)

                def gate(p, u, o):
                    dve.wait_ge(mm_done, (l * LU + G0 + p * G_U + u) * 2 + o + 1 + MM_CREDIT)
                    dve.wait_ge(m_ready, (l * 4 + p) * 2 + o + 1)
                    nc.vector.tensor_tensor((sA, sB)[u][:, o, :], pj[o][:], rstd_all[:],
                                            ALU.mult).then_inc(bank_free[o], 1)

                def merge(p):
                    J = l * 4 + p
                    n = l * LU + G0 + p * G_U
                    q = l * LQ + G0 - P0 + p * G_U
                    for u, dst in ((2, sB), (3, sA)):
                        for o in range(2):
                            dve.wait_ge(gate_sigmoid, J * 4 + 4)
                            dve.wait_ge(mm_done, (n + u) * 2 + o + 1 + MM_CREDIT)
                            nc.vector.tensor_tensor(dst[:, o, :], pj[o][:], dst[:, o, :],
                                                    ALU.mult).then_inc(bank_free[o], 1)
                    for o in range(2):
                        dve.wait_ge(bank_free[o], q + 4 + BANK_CREDIT)
                        nc.vector.tensor_tensor(sA[:, o, :], sA[:, o, :], sB[:, o, :], ALU.add).then_inc(merged, 1)
                    for o in range(2):
                        at_ = 2 * p + o
                        if isinstance(p, int):
                            mh, ml = m_hi[:, at_, :], m_lo[:, at_, :]
                        else:
                            mh, ml = (m[:, bass.ds(at_, 1), :].rearrange("p k s -> p (k s)") for m in (m_hi, m_lo))
                        dve.wait_ge(merged, J * 2 + o + 1)
                        nc.vector.tensor_scalar(mh, sA[:, o, :], 1.0, None, ALU.mult).then_inc(m_hi_done, 1)
                        dve.wait_ge(m_hi_done, J * 2 + o + 1)
                        nc.vector.tensor_tensor(ml, sA[:, o, :], mh, ALU.subtract).then_inc(m_ready, 1)

                gate(0, 0, 0)
                factors()
                u_scale(0)
                u_scale(1)
                gate(0, 0, 1)
                u_scale(2)
                u_scale(3)
                split_z(range(0, 4))
                gate(0, 1, 0)
                split_z(range(4, 8))
                gate(0, 1, 1)
                y_add(0)
                y_add(1)
                y_split(0)
                y_split(1)
                y_add(2)
                y_add(3)
                y_split(2)
                y_split(3)
                with dve.Fori(0, 3) as p:
                    merge(p)
                    for u in range(2):
                        for o in range(2):
                            gate(p + 1, u, o)
                merge(3)
                def x_add(n, t, o):
                    dve.wait_ge(mm_done, n * 2 + o + 1 + MM_CREDIT)
                    nc.vector.tensor_tensor(x[:, t, :], pj[o][:], x[:, t, :], ALU.add).then_inc(bank_free[o], 1)

                dve.wait_ge(gain_set, l + 1)
                for u in range(4):
                    for o in range(2):
                        x_add(l * LU + O0 + u, 2 * u + o, o)
                        dve.wait_ge(bank_free[o], l * LQ + O0 - P0 + u + 1 + BANK_CREDIT)
                        scale_and_split(2 * l + 1, 2 * u + o, gain[:, 0, :])
                def relu_square(c, u, o):
                    t = 2 * u + o if u < 8 else 8 + o
                    dve.wait_ge(bank_free[o], l * LQ + M0 - P0 + c * M_U + u + 1 + BANK_CREDIT)
                    nc.vector.tensor_tensor(relu2[:, o, :], relu[:, o, :], rstd_all[:], ALU.mult).then_inc(relu_scaled, 1)
                    dve.wait_ge(relu_scaled, (l * CH + c) * 8 + t + 1)
                    nc.vector.tensor_tensor(relu2[:, o, :], relu2[:, o, :], relu[:, o, :],
                                            ALU.mult).then_inc(relu2_done, 1)
                    dve.wait_ge(u_hi_done, (l * CH + c) * 8 + t + 1)
                    nc.vector.tensor_tensor(u_lo[:, t % 8, :], relu2[:, o, :], u_hi[:, t % 8, :],
                                            ALU.subtract).then_inc(u_ready, 1)

                for k in range(KT):
                    mm = nc.vector.tensor_scalar(gdiag[:, k, :], ident[:], gain[:, 1, k:k + 1], None, ALU.mult)
                mm.then_inc(gdiag_done, 1)
                rms(2 * l + 1, squared=True)
                rms_spread(2 * l + 1)
                for o in range(2):
                    relu_square(0, 0, o)
                with dve.Fori(0, CH - 1) as c:
                    for u in (1, 2, 3, 4, 5, 6, 7, 8):
                        for o in range(2):
                            if 4 <= u < 8:
                                x_add(l * LU + M0 + c * M_U + u, 2 * (u - 4) + o, o)
                            else:
                                relu_square(c, u, o)
                for u in (1, 2, 3):
                    for o in range(2):
                        relu_square(CH - 1, u, o)
                for u in (4, 5, 6, 7):
                    for o in range(2):
                        t = 2 * (u - 4) + o
                        x_add(l * LU + M0 + (CH - 1) * M_U + u, t, o)
                        dve.wait_ge(bank_free[o], l * LQ + M0 - P0 + (CH - 1) * M_U + u + 1 + BANK_CREDIT)
                        scale_and_split(2 * l + 2, t, gain[:, 1, :])
            dve.wait_ge(std_done, 2 * DEPTH + 1)
            nc.vector.reciprocal(rstd[:, 0:TB], std[:, 0:TB]).then_inc(rstd_done, 1)
            dve.wait_ge(rstd_done, 2 * DEPTH + 1)
            for b in range(TB):
                dve.wait_ge(f_turned, b + 1)
                nc.vector.tensor_scalar(stage[:, b, S:D], fbank[b][1], rstd[:, b:b + 1], None,
                                        ALU.mult).then_inc(f_staged[1], 1)

        @block.tensor
        def _(pe):
            pe.sem_inc(mm_done, MM_CREDIT)
            pe.sem_inc(ret_mm, 2)
            pe.wait_ge(ident_in, 16)
            pe.wait_ge(const_set, 3)
            for k in range(KT):
                if k % (KT // 2) == 0:
                    pe.wait_ge(x_in[k // (KT // 2)], 16)
                for b in range(TB):
                    last = nc.tensor.transpose(xbank[k][:, b * P:(b + 1) * P], x_nat[:, b, k * P:(k + 1) * P],
                                               ident[:])
                last.then_inc(x_turned, 1)
            pe.wait_ge(x_init, TB)

            def mean(J, by_residue_too=True):
                pe.wait_ge(sum_done, (J + 1) * (KT - 1))
                for b in range(TB):
                    mm = nc.tensor.matmul(rb[:, b:b + 1], ssum[:, b * P:(b + 1) * P], inv_d[:], start=True, stop=True)
                for b in range(TB if by_residue_too else 0):
                    mm = nc.tensor.matmul(rb[:, TB + b:TB + b + 1], by_residue(ssum[:])[:, b], inv_d[:],
                                          start=True, stop=True)
                mm.then_inc(mean_done, 1)

            def spread(J):
                pe.wait_ge(diag_done, J + 1)
                for b in range(TB):
                    mm = nc.tensor.matmul(rb[:, b * P:(b + 1) * P], ones[:], diag[:, b, :], start=True, stop=True)
                mm.then_inc(spread_done, 1)

            def weights(n, half=1):
                pe.wait_ge(lo_done, n * 2 + half + 1 + UNIT_CREDIT)

            def three(out, s, wc, acts, first, last):
                nc.tensor.matmul(out, w_hi[s][:, wc], acts[0], start=first, stop=False)
                nc.tensor.matmul(out, w_hi[s][:, wc], acts[1], start=False, stop=False)
                return nc.tensor.matmul(out, w_lo[s][:, wc], acts[0], start=False, stop=last)

            def tile_half(s, o, acts, ks, kt=KT, ready=None):
                for k in ks:
                    if ready:
                        ready(k)
                    mm = three(pj[o][:], s, slice(k * 256 + o * P, k * 256 + o * P + P),
                               (acts[0][:, k, :], acts[1][:, k, :]), k == 0, k == kt - 1)
                if ks[-1] == kt - 1:
                    mm.then_inc(mm_done, 1)

            def unit(n, q, s, acts, kt=KT, ready=None, behind=(None, None)):
                def first(k):
                    if k % (KT // 2) == 0:
                        weights(n, k // (KT // 2))
                    if ready:
                        ready(k)

                for o in range(2):
                    pe.wait_ge(bank_free[o], q + BANK_CREDIT)
                    if o == 1 and kt < KT:
                        weights(n)
                    tile_half(s, o, acts, range(kt), kt, first if o == 0 else None)
                    if behind[o]:
                        behind[o]()

            h = (h_hi, h_lo)
            with pe.Fori(0, DEPTH) as l:
                def values_half(g, u):
                    for kk in range(4):
                        if kk % 2 == 0:
                            weights(l * LU + V0 + g * V_U + u, kk // 2)
                        k = 4 * u + kk
                        if g == 0:
                            pe.wait_ge(h_ready, l * 2 * KT + k + 1)
                        w = slice(kk * 512, kk * 512 + 512)
                        for b in range(TB):
                            if k == 0:
                                pe.wait_ge(v_out, (l * GROUPS + g) * TB + b + 1)
                            if g == 0:
                                hh, hl = h_hi[:, k, b * P:(b + 1) * P], h_lo[:, k, b * P:(b + 1) * P]
                            else:
                                hh, hl = by_residue(h_hi[:, k, :])[:, b], by_residue(h_lo[:, k, :])[:, b]
                            nc.tensor.matmul(vbank[b], hh, w_hi[u][:, w], start=(k == 0), stop=False)
                            nc.tensor.matmul(vbank[b], hh, w_lo[u][:, w], start=False, stop=False)
                            mm = nc.tensor.matmul(vbank[b], hl, w_hi[u][:, w], start=False, stop=(k == KT - 1))
                            if k == KT - 1 and b < TB - 1:
                                mm.then_inc(v_done, 1)
                    mm.then_inc(mm_done, 2)

                values_half(0, 0)
                for k in range(4, KT):
                    pe.wait_ge(h_ready, l * 2 * KT + k + 1)
                mean(2 * l)
                values_half(0, 1)
                for g in range(1, GROUPS):
                    values_half(g, 0)
                    values_half(g, 1)
                spread(2 * l)
                with pe.Fori(0, PAIRS) as i:
                    J = l * PAIRS + i
                    n = l * LU + P0 + i * P_U
                    q = l * LQ + i * P_U

                    off = [[pe.snap(i * P + (g * AW + hh * DH)) for hh in range(2)] for g in range(GROUPS)]

                    def scores(j):
                        if j == 0:
                            pe.wait_ge(rot_out, J * 8 + 6 + 1)
                            pe.wait_ge(v_out, l * GROUPS * TB + (GROUPS + 1) * TB)
                        else:
                            pe.wait_ge(att_masked, (J * 8 + 2 * j) * 2)
                        Q, c = slice(j * P, j * P + P), keys(0, 2 * j)
                        own = slice((j + 1) * P - (c.stop - c.start), (j + 1) * P)
                        for g, to, k in ((0, c, own), (1, slice(2 * P, 3 * P), Q), (2, slice(3 * P, 4 * P), Q)):
                            for hh in range(2):
                                rows = slice(hh * DH, hh * DH + DH)
                                mm = nc.tensor.matmul(sc[:, hh * S + to.start:hh * S + to.stop], qk[rows, 2 * g, Q],
                                                      qk[rows, 2 * g + 1, k], start=True, stop=True)
                                if g == GROUPS - 1:
                                    mm.then_inc(att_qk, 1)

                    def turn(b):
                        pe.wait_ge(att_exp, (J * 8 + b + 1) * 2)
                        if b >= 1:
                            pe.wait_ge(att_probT, J * 8 + b)
                        for j in range(keys(0, b).start // P, 4):
                            mm = nc.tensor.transpose(pt[:, j * P:(j + 1) * P], prob[:, j * P:(j + 1) * P], ident[:])
                        mm.then_inc(att_turned, 1)

                    def values(b):
                        j, hh = b // 2, b % 2
                        if b == 0:
                            pe.wait_ge(u_out, J * 2 + 2)
                        pe.wait_ge(att_probT, J * 8 + b + 1)
                        for side in range(2):
                            out = yo[:, side * S + j * P + hh * DH:side * S + j * P + hh * DH + DH]
                            terms = [(0, 0, j - 1), (1, 0, j)][0 if j else 1:] if side == 0 else [(2, 1, j), (3, 2, j)]
                            for t, (blk, g, vb) in enumerate(terms):
                                mm = nc.tensor.matmul(out, probT[:, blk * P:(blk + 1) * P],
                                                      vA[:, vb, bass.ds(off[g][hh], DH)],
                                                      start=(t == 0), stop=(t == len(terms) - 1))
                        mm.then_inc(att_pv, 1)

                    def st(j):
                        if j == 0:
                            pe.wait_ge(rot_out, J * 8 + 8 + 1)
                            pe.wait_ge(ret_std, J + 1)
                            pe.wait_ge(rstd_all_done, 2 * l + 1)
                        else:
                            pe.wait_ge(st_out, J * TB + j + 1)
                        nc.tensor.matmul(rb[:, 0:S - j * P], qkR[:, 1, j * P:(j + 1) * P], qkR[:, 0, j * P:S],
                                         start=True, stop=True).then_inc(st_mm, 1)

                    def ret(e):
                        if e == 0:
                            pe.wait_ge(st_out, J * TB + TB + 1)
                            for o in range(2):
                                pe.wait_ge(bank_free[o], q + 5 + BANK_CREDIT)
                        else:
                            pe.wait_ge(ret_out, J * 2 + 1)
                            pe.wait_ge(ret_sq, J * 2 + 1)
                        for j in range(TB):
                            w = S - j * P
                            mm = nc.tensor.matmul(rb[:, j * P:S], vR[:, j, e * P:(e + 1) * P],
                                                  ST[:, st0[j]:st0[j] + w], start=(j == 0), stop=(j == TB - 1))
                        mm.then_inc(ret_mm, 1)

                    for u in range(GROUPS):
                        unit(n + u, q + u, u % 2, h)
                    for s in range(12):
                        u, o, half = 3 + s // 4, s // 2 % 2, s % 2
                        sl = u % 2
                        if s % 4 == 0:
                            weights(n + u, 1 if u == 4 else 0)
                        if s % 4 == 1 and u != 4:
                            weights(n + u, 1)
                        if half == 0:
                            pe.wait_ge(bank_free[o], q + u + BANK_CREDIT)
                        if u != 4:
                            tile_half(sl, o, h, range(4 * half, 4 * half + 4))
                        else:
                            b = 2 * o + half
                            out = pj[o][:, half * RV:(half + 1) * RV]
                            for k in range(KT):
                                w = slice(k * 256, k * 256 + 256)
                                hh, hl = h_hi[:, k, b * P:(b + 1) * P], h_lo[:, k, b * P:(b + 1) * P]
                                nc.tensor.matmul(out, hh, w_hi[sl][:, w], start=(k == 0), stop=False)
                                nc.tensor.matmul(out, hh, w_lo[sl][:, w], start=False, stop=False)
                                mm = nc.tensor.matmul(out, hl, w_hi[sl][:, w], start=False, stop=(k == KT - 1))
                            if half == 1:
                                mm.then_inc(mm_done, 1)
                        if 3 <= s < 11:
                            values(s - 3)
                        if 2 <= s < 10:
                            turn(s - 2)
                        if s % 2 == 1 and s < 8:
                            scores(s // 2)
                        if 5 <= s < 9:
                            st(s - 5)
                        if 9 <= s < 11:
                            ret(s - 9)
                    pe.wait_ge(ret_sum, J + 1)
                    pe.wait_ge(ret_out, J * 2 + 2)
                    nc.tensor.matmul(rb[:], ones[:], rcos[:], start=True, stop=True).then_inc(ret_mean, 1)
                def y_turn(j):
                    pe.wait_ge(u_scaled, (l * PAIRS + j + 1) * 2)
                    if j >= 2:
                        pe.wait_ge(y_summed, l * PAIRS + j - 1)
                    own, by_res = ybank[j % 2]
                    for b in range(TB):
                        nc.tensor.transpose(own[:, b * P:(b + 1) * P], U[:, 0, b, j * P:(j + 1) * P], ident[:])
                    for r in range(TB):
                        mm = nc.tensor.transpose(by_residue(by_res)[:, r], U[:, 1, r, j * P:(j + 1) * P], ident[:])
                    mm.then_inc(y_turned, 1)

                def gates(p, behind=(None, None)):
                    n = l * LU + G0 + p * G_U
                    q = l * LQ + G0 - P0 + p * G_U
                    unit(n, q, 0, h)
                    unit(n + 1, q + 1, 1, h, behind=(None, behind[0]))
                    unit(n + 2, q + 2, 0, (z_hi, z_lo), KT, lambda k: pe.wait_ge(split_done, l * KT + k + 1),
                         (behind[1], None))
                    unit(n + 3, q + 3, 1, (y_hi, y_lo), KA, lambda k: pe.wait_ge(y_ready, l * PAIRS + k + 1))

                def turn_two(j):
                    y_turn(j)
                    y_turn(j + 1)

                gates(0, (lambda: turn_two(0), lambda: turn_two(2)))
                with pe.Fori(1, 4) as p:
                    gates(p)
                for u in range(4):
                    unit(l * LU + O0 + u, l * LQ + O0 - P0 + u, u % 2, (m_hi, m_lo), KT,
                         (lambda k: pe.wait_ge(m_ready, l * KT + k + 1 + 2)) if u == 0 else None)

                def mlp(c, us, ready=None, behind=(None, None)):
                    n = l * LU + M0 + c * M_U
                    q = l * LQ + M0 - P0 + c * M_U
                    for u in us:
                        acts = h if u < 4 or u == 8 else (u_hi, u_lo)
                        wait_u = lambda k: pe.wait_ge(u_ready, (l * CH + c) * 8 + k + 1)
                        unit(n + u, q + u, u % 2, acts, KT, wait_u if u == 4 else ready, behind)

                mlp(0, (0,), lambda k: pe.wait_ge(h_ready, l * 2 * KT + KT + k + 1),
                    (lambda: mean(2 * l + 1), lambda: spread(2 * l + 1)))
                with pe.Fori(0, CH - 1) as c:
                    mlp(c, range(1, 9))
                mlp(CH - 1, range(1, 8))
            pe.wait_ge(gdiag_done, DEPTH)
            for b in range(TB):
                if b == 2:
                    mean(2 * DEPTH, by_residue_too=False)
                if b == 3:
                    for staged in f_staged:
                        pe.wait_ge(staged, 1)
                for k in range(KT):
                    if b == 0 and k % 2 == 0:
                        for o in range(2):
                            pe.wait_ge(bank_free[o], DEPTH * LQ - KT // 2 + k // 2 + 1 + BANK_CREDIT)
                    mm = nc.tensor.matmul(fbank[b][k // TB][:, k % TB * P:(k % TB + 1) * P],
                                          x[:, k, b * P:(b + 1) * P], gdiag[:, k, :], start=True, stop=True)
                mm.then_inc(f_turned, 1)


def constants(S, D):
    import numpy as np

    f = np.float32
    pos = np.arange(S, dtype=f)

    def tables(half, base):
        inv = (f(1.0) / (f(base) ** (np.arange(half, dtype=f) / f(half)))).astype(f)
        ang = (pos[None, :] * inv[:, None]).astype(f)
        return np.cos(ang).astype(f), np.sin(ang).astype(f)

    cosA, sinA = np.ones((P, S), f), np.zeros((P, S), f)
    c, s = tables(8, 500000.0)
    for h in (0, 64):
        cosA[h:h + 8], cosA[h + 8:h + 16] = c, c
        sinA[h:h + 8], sinA[h + 8:h + 16] = -s, s
    c, s = tables(64, 10000.0)
    cosR, sinR = np.concatenate([c, c]), np.concatenate([-s, s])

    lg = np.log1p(-(f(2.0) ** (f(-5.0) - np.arange(4, dtype=f)))).astype(f)
    diff = (np.arange(S)[None, :] - np.arange(P)[:, None]).astype(f)
    decay = np.exp(np.maximum(diff, f(0))[:, None, :] * lg[None, :, None])
    decay = (np.where(diff[:, None, :] >= 0, decay, f(0)) * f(P ** -0.5)).astype(f)

    m = np.arange(P)
    back = m[:, None] + P - np.arange(2 * P)[None, :]
    d = m[:, None] - m[None, :]
    seen = np.concatenate([(back >= 0) & (back <= P), d >= 0, (d >= 0) & (d % 4 == 0)], axis=1)
    mask = np.where(seen, f(0), f(-1e30)).astype(f)
    tables = np.stack([cosA, sinA, cosR, sinR], axis=1).astype(f)
    return {"tables": tables, "decay": np.ascontiguousarray(decay.transpose(1, 0, 2)),
            "mask": mask, "ident": np.eye(P, dtype=f)}


_INS = ["x", "w_in", "w_a", "w_b", "w_o", "w_up", "w_down"]


def kernel(**inputs):
    import numpy as np
    import concourse.bacc as bacc
    from concourse.bass_utils import run_bass_kernel_spmd

    nc = bacc.Bacc("TRN2", target_bir_lowering=False, num_devices=1)
    arrays = {n: np.ascontiguousarray(inputs[n]) for n in _INS}
    shape = arrays["x"].shape
    norms = [g for pair in zip(inputs["mix_norm"], inputs["ffn_norm"]) for g in pair] + [inputs["final_norm"]]
    gains = np.stack([np.asarray(g) for g in norms]).reshape(len(norms), -1, P)
    arrays["gains"] = np.ascontiguousarray(gains.transpose(2, 0, 1))
    arrays.update(constants(shape[1], shape[2]))
    feeds, aps = {}, {}
    for name, v in arrays.items():
        feeds[f"in_{name}"] = v
        aps[name] = nc.dram_tensor(f"in_{name}", v.shape, mybir.dt.from_np(v.dtype), kind="ExternalInput").ap()
    aps["out"] = nc.dram_tensor("out_x", shape, F32, kind="ExternalOutput").ap()
    trunk(nc, aps)
    r = run_bass_kernel_spmd(nc, [feeds], core_ids=[0])
    return r.results[0]["out_x"]
```
